# Optimizing a Trainium2 kernel written in Bass

```python
import jax, jax.numpy as jnp
from jax import lax
import numpy as np

D_MODEL = 1024
BATCH = 1
SEQ = 1024
DEPTH = 1

CHUNK = 64
GMLP_BLOCK = 128
GMLP_WIDTH = D_MODEL
GMLP_GROUPS = 8
GMLP_GROUP_DIM = GMLP_WIDTH // GMLP_GROUPS
CONV_WIDTH = D_MODEL
CONV_K = 3
PEER_HEADS = 8
PEER_KEY_DIM = 256
PEER_HALF = PEER_KEY_DIM // 2
PEER_N_KEYS = 128
PEER_N_EXPERTS = PEER_N_KEYS * PEER_N_KEYS
PEER_TOPK = 16
PEER_TOKEN_BLOCK = 128
IN_COLS = 2 * GMLP_WIDTH + 3 * CONV_WIDTH + 2 * D_MODEL
DEEPNORM_ALPHA = (2.0 * DEPTH) ** 0.25
DEEPNORM_BETA = (8.0 * DEPTH) ** -0.25
LN_EPS = 1e-5

kernel_name = "hybrid_gmlp_shortconv_peer_deepnorm_adaln"

def _layer_norm(x, g=None, b=None):
    xf = x.astype(jnp.float32)
    mu = jnp.mean(xf, axis=-1, keepdims=True)
    var = jnp.mean(jnp.square(xf - mu), axis=-1, keepdims=True)
    y = (xf - mu) * lax.rsqrt(var + LN_EPS)
    if g is not None:
        y = y * g.astype(jnp.float32) + b.astype(jnp.float32)
    return y.astype(x.dtype)

def _adaln(x, shift, scale):
    return _layer_norm(x) * (1 + scale[:, None, :]) + shift[:, None, :]

def _gmlp_mixer(u, v, ln_g, ln_b, w_s, b_s):
    bsz, seq, _ = v.shape
    u = jax.nn.gelu(u)
    v = _layer_norm(jax.nn.gelu(v), ln_g, ln_b)
    pos = jnp.arange(GMLP_BLOCK)
    mask = (pos[None, :] // CHUNK) <= (pos[:, None] // CHUNK)
    w = jnp.where(mask[None], w_s, 0)
    vb = v.reshape(bsz, seq // GMLP_BLOCK, GMLP_BLOCK, GMLP_GROUPS, GMLP_GROUP_DIM)
    mixed = jnp.einsum('gij,bnjgc->bnigc', w, vb) + b_s.T[None, None, :, :, None]
    return u * mixed.reshape(bsz, seq, GMLP_WIDTH)

def _short_conv_mixer(g_b, g_c, z, conv_w):
    seq = z.shape[1]
    zc = jnp.pad(g_c * z, ((0, 0), (CONV_K - 1, 0), (0, 0)))
    y = sum(zc[:, k:k + seq] * conv_w[k] for k in range(CONV_K))
    return g_b * y

def _peer(h, w_q, sub_keys, expert_u, expert_v):
    bsz, seq, d = h.shape
    xt = h.reshape((bsz * seq) // PEER_TOKEN_BLOCK, PEER_TOKEN_BLOCK, d)

    def block(xb):
        t = xb.shape[0]
        q = (xb @ w_q).reshape(t, PEER_HEADS, 2, PEER_HALF)
        s = jnp.einsum('thpd,hpkd->thpk', q, sub_keys).astype(jnp.float32)
        s1, i1 = lax.top_k(s[:, :, 0], PEER_TOPK)
        s2, i2 = lax.top_k(s[:, :, 1], PEER_TOPK)
        cand_s = (s1[..., :, None] + s2[..., None, :]).reshape(t, PEER_HEADS, PEER_TOPK * PEER_TOPK)
        cand_i = (i1[..., :, None] * PEER_N_KEYS + i2[..., None, :]).reshape(t, PEER_HEADS, PEER_TOPK * PEER_TOPK)
        top_s, sel = lax.top_k(cand_s, PEER_TOPK)
        idx = jnp.take_along_axis(cand_i, sel, axis=-1)
        gate = jax.nn.softmax(top_s, axis=-1).astype(xb.dtype)
        u = jnp.take(expert_u, idx, axis=0)
        act = jax.nn.gelu(jnp.einsum('thkd,td->thk', u, xb))
        v = jnp.take(expert_v, idx, axis=0)
        return jnp.einsum('thk,thkd->td', gate * act, v)

    return lax.map(block, xt).reshape(bsz, seq, d)

def setup_inputs(seed: int = 0) -> dict:
    key = jax.random.key(seed)
    ks = jax.random.split(key, 24)
    nrm = lambda k, shape, s: jax.random.normal(k, shape, jnp.float32) * s
    L, D = DEPTH, D_MODEL
    gate_bias = jnp.concatenate([jnp.zeros((2 * D,)), jnp.ones((D,))] * 2)
    return {
        "x": nrm(ks[0], (BATCH, SEQ, D), 1.0),
        "c": nrm(ks[1], (BATCH, D), 1.0),
        "w_cond": nrm(ks[2], (L, D, 6 * D), 0.5 * D ** -0.5),
        "b_cond": gate_bias[None] + nrm(ks[3], (L, 6 * D), 0.02),
        "w_in": nrm(ks[4], (L, D, IN_COLS), D ** -0.5),
        "gmlp_ln_g": 1.0 + nrm(ks[5], (L, GMLP_WIDTH), 0.05),
        "gmlp_ln_b": nrm(ks[6], (L, GMLP_WIDTH), 0.02),
        "w_spatial": nrm(ks[7], (L, GMLP_GROUPS, GMLP_BLOCK, GMLP_BLOCK), GMLP_BLOCK ** -0.5),
        "b_spatial": 1.0 + nrm(ks[8], (L, GMLP_GROUPS, GMLP_BLOCK), 0.1),
        "conv_w": nrm(ks[9], (L, CONV_K, CONV_WIDTH), CONV_K ** -0.5),
        "p_a": nrm(ks[10], (L, GMLP_WIDTH, D), DEEPNORM_BETA * GMLP_WIDTH ** -0.5),
        "p_b": nrm(ks[11], (L, CONV_WIDTH, D), DEEPNORM_BETA * CONV_WIDTH ** -0.5),
        "w_o": nrm(ks[12], (L, D, D), DEEPNORM_BETA * D ** -0.5),
        "ln1_g": 1.0 + nrm(ks[13], (L, D), 0.05),
        "ln1_b": nrm(ks[14], (L, D), 0.02),
        "w_q_peer": nrm(ks[15], (L, D, PEER_HEADS * PEER_KEY_DIM), D ** -0.5),
        "sub_keys": nrm(ks[16], (L, PEER_HEADS, 2, PEER_N_KEYS, PEER_HALF), PEER_HALF ** -0.5),
        "expert_u": nrm(ks[17], (L, PEER_N_EXPERTS, D), D ** -0.5),
        "expert_v": nrm(ks[18], (L, PEER_N_EXPERTS, D), DEEPNORM_BETA),
        "ln2_g": 1.0 + nrm(ks[19], (L, D), 0.05),
        "ln2_b": nrm(ks[20], (L, D), 0.02),
    }

def reference(x, c, w_cond, b_cond, w_in, gmlp_ln_g, gmlp_ln_b, w_spatial, b_spatial,
              conv_w, p_a, p_b, w_o, ln1_g, ln1_b, w_q_peer, sub_keys, expert_u,
              expert_v, ln2_g, ln2_b):
    o_v = GMLP_WIDTH
    o_b = 2 * GMLP_WIDTH
    o_c = o_b + CONV_WIDTH
    o_z = o_c + CONV_WIDTH
    o_ga = o_z + CONV_WIDTH
    o_gb = o_ga + D_MODEL
    for l in range(DEPTH):
        mod = jax.nn.silu(c) @ w_cond[l] + b_cond[l]
        sh1, sc1, g1, sh2, sc2, g2 = jnp.split(mod, 6, axis=-1)

        h = _adaln(x, sh1, sc1)
        proj = h @ w_in[l]
        y_a = _gmlp_mixer(proj[..., :o_v], proj[..., o_v:o_b], gmlp_ln_g[l], gmlp_ln_b[l],
                          w_spatial[l], b_spatial[l])
        y_b = _short_conv_mixer(proj[..., o_b:o_c], proj[..., o_c:o_z], proj[..., o_z:o_ga],
                                conv_w[l])
        merged = (jax.nn.sigmoid(proj[..., o_ga:o_gb]) * (y_a @ p_a[l])
                  + jax.nn.sigmoid(proj[..., o_gb:]) * (y_b @ p_b[l]))
        mix = merged @ w_o[l]
        x = _layer_norm(DEEPNORM_ALPHA * x + g1[:, None, :] * mix, ln1_g[l], ln1_b[l])

        h2 = _adaln(x, sh2, sc2)
        ffn = _peer(h2, w_q_peer[l], sub_keys[l], expert_u[l], expert_v[l])
        x = _layer_norm(DEEPNORM_ALPHA * x + g2[:, None, :] * ffn, ln2_g[l], ln2_b[l])
    return x


_drawn_inputs = setup_inputs


def setup_inputs(seed=0):
    import zlib

    import numpy as np

    out = dict(_drawn_inputs(seed))
    spreads = {}
    factors = {'gmlp_ln_b': 4.299, 'ln2_b': 2.951}
    for name, (base, spread) in spreads.items():
        noise = np.random.default_rng([zlib.crc32(name.encode()), seed]).standard_normal(out[name].shape)
        drawn = base * np.exp(spread * noise) if base else spread * noise
        out[name] = __import__('jax').numpy.asarray(drawn.astype(out[name].dtype))
    for name, factor in factors.items():
        out[name] = (out[name] * factor).astype(out[name].dtype)
    return out
```

```python
from contextlib import ExitStack

import numpy as np

import concourse.bass as bass
from concourse import mybir

ALU = mybir.AluOpType
ACT = mybir.ActivationFunctionType
F32 = mybir.dt.float32
F16 = mybir.dt.float16
U32 = mybir.dt.uint32
I32 = mybir.dt.int32
AX_X = mybir.AxisListType.X

P = 128
D = 1024
S = 1024
KD = D // P
NB = S // P
GROUPS = 8
HEADS = 8
NKEYS = 128
TOPK = 16
HT = 512
UC = 256
ALPHA = 2.0 ** 0.25
EPS = 1e-5
WS = 256.0
AS = 16.0
DESCALE = 1.0 / (WS * AS)
GS = 4096.0
LOWEST = -3.0e38

NCOND = 6 * D // UC
N_V, N_CONV, N_U, N_MERGE, N_O, N_Q = 4, 12, 4, 16, 4, 8
U_V = 0
U_CONV = U_V + N_V
U_U = U_CONV + N_CONV
U_MERGE = U_U + N_U
U_O = U_MERGE + N_MERGE
U_Q = U_O + N_O
U_PEER = U_Q + N_Q
NGRP = 32
T_V = 0
T_CONV = T_V + 8 * N_V
T_U = T_CONV + 4 * N_CONV
T_MERGE = T_U + 4 * N_U
T_O = T_MERGE + 4 * N_MERGE
T_Q = T_O + 8 * N_O
T_PEER = T_Q + 4 * N_Q
A_COND = 0
A_HT = A_COND + NCOND
A_MIX = A_HT + 16
A_H2T = A_MIX + 16
A_IDX = A_H2T + 16
A_END = A_IDX + 6
E_CONV = 1
E_U = E_CONV + 8
E_MERGE = E_U + 4
E_END = E_MERGE + 8


def trunk_layer(nc, x, c_col, w_cond, b_cond, w_front, ln_g, ln_b, w_spat, b_spat, conv_w,
                ln1_g, ln1_b, keys_t, u_units, expert_v, ln2_g, ln2_b, out):
    with ExitStack() as ctx:
        def sb(name, shape, dt=F32):
            return ctx.enter_context(nc.sbuf_tensor(name, shape, dt))

        def sem(name):
            return ctx.enter_context(nc.semaphore(name))

        stage = sb("stage", [P, 2, 2048])
        w_hi = sb("w_hi", [P, 2, 2048], F16)
        w_lo = sb("w_lo", [P, 2, 2048], F16)
        h_hi = sb("h_hi", [P, KD, S], F16)
        h_lo = sb("h_lo", [P, KD, S], F16)
        R1 = sb("R1", [P, 8192])
        R2 = sb("R2", [P, 8192])
        R3 = sb("R3", [P, 8192 + 2052 + 2048 + 2048])
        par = sb("par", [P, 3, D])
        bs_b = sb("bs_b", [P, GROUPS, P])
        ident = sb("ident", [P, P])
        iota_i = sb("iota_i", [P, P], I32)
        iota16b = sb("iota16b", [P, P], F16)
        iota_f = sb("iota_f", [P, TOPK])
        cw = sb("cw", [P, KD, 3])
        ccol = sb("ccol", [P, KD])
        cth = sb("cth", [P, KD])
        stats = sb("stats", [P, NB, 2, 6])
        mv = sb("mv", [P, NB, 2])
        vare = sb("vare", [P, NB])
        std = sb("std", [P, NB])
        rstd = sb("rstd", [P, NB])

        def view(region, at, n, dt=F32):
            v = region[:, at:at + n]
            return v.bitcast(dt) if dt != F32 else v

        def v3(ap, a):
            return ap.rearrange("p (a b) -> p a b", a=a)

        xt = v3(view(R1, 0, 8192), NB)
        ya_hi = v3(view(R1, 0, 4096, F16), KD)
        ya_lo = v3(view(R1, 4096, 4096, F16), KD)
        yb_hi = v3(view(R2, 0, 4096, F16), KD)
        yb_lo = v3(view(R2, 4096, 4096, F16), KD)
        x2 = v3(view(R2, 0, 8192), NB)
        mod = view(R3, 0, 6144)
        crep = v3(view(R3, 6144, 1024), KD)
        mixb = v3(view(R3, 0, 8192), GROUPS)
        m_hi = v3(view(R3, 0, 4096, F16), KD)
        m_lo = v3(view(R3, 4096, 4096, F16), KD)
        evA = v3(view(R3, 8192, 2052), 2)
        evB = v3(view(R3, 10244, 2048), 2)
        evC = v3(view(R3, 12292, 2048), 2)
        evAd = evA[:, :, 2:2 + S]
        sh2b = view(R3, 10244, D)
        sc2b = view(R3, 12292, D)
        ws_t = v3(par[:, 2, :], GROUPS)
        qb = [v3(view(R2, 2048 * i, 2048), 2) for i in range(2)]
        sc = [view(R2, 4096 + 2048 * i, 2048).rearrange("p (b h k) -> p b h k", b=NB, h=2) for i in range(2)]
        keys_sb = par[:, 0:2, :].rearrange("p a (g k) -> p (a g) k", k=NKEYS)
        sc2 = view(R3, 0, 2048).rearrange("p (b h k) -> p b h k", b=NB, h=2)
        cand = view(R3, 2048, 2048).rearrange("p (b i j) -> p b i j", b=NB, i=TOPK)
        cand2 = v3(view(R3, 4096, 2048), NB)
        cmp_t = v3(view(R3, 6144, 2048), NB * TOPK)
        vals = view(R3, 8192, 256).rearrange("p (b h k) -> p b h k", b=NB, h=2)
        idx = view(R3, 8448, 256, U32).rearrange("p (b h k) -> p b h k", b=NB, h=2)
        idxf = view(R3, 8704, 256).rearrange("p (b h k) -> p b h k", b=NB, h=2)
        sel = v3(view(R3, 8960, 128, U32), NB)
        sel_a = view(R3, 9088, 128, U32)
        sel_b = view(R3, 9216, 128, U32)
        sel_af = view(R3, 9344, 128)
        sel_bf = view(R3, 9472, 128)
        tops = v3(view(R3, 9600, 128), NB)
        rsum = view(R3, 9728, 64)
        rinv = view(R3, 9792, 64)
        i1_all = view(R3, 10244, 1024).rearrange("p (b h k) -> p b h k", b=NB, h=HEADS)
        i2_all = view(R3, 11268, 1024).rearrange("p (b h k) -> p b h k", b=NB, h=HEADS)
        s_all = view(R3, 12292, 1024).rearrange("p (b h k) -> p b h k", b=NB, h=HEADS)
        i1_t = view(R3, 0, 1024)
        i2_t = view(R3, 1024, 1024)
        g_t = view(R3, 2048, 1024)
        glo_t = view(R3, 3072, 1024)
        g16 = view(R3, 4096, 512, F16)
        oh = view(R3, 4608, 4 * 768, F16).rearrange("p (r t c k) -> p r t c k", r=4, t=4, c=3)
        gbuf = [view(R2, 4096 * i, 4096).rearrange("p (k t) -> p k t", t=32) for i in range(2)]
        A_t = v3(view(R2, 0, 4096), 4)
        G_t = view(R2, 4096, 4096).rearrange("p (n j t) -> p n j t", n=32, j=4)
        c_hi = v3(view(R3, 0, 2048, F16), 4)
        c_lo = v3(view(R3, 2048, 2048, F16), 4)
        acc = v3(view(R3, 4096, 8192), NB)

        psU = [ctx.enter_context(nc.psum_tensor(f"psU{i}", [P, 512], F32)) for i in range(4)]
        psX = [ctx.enter_context(nc.psum_tensor(f"psX{i}", [P, 512], F32)) for i in range(4)]

        mod_dram = nc.dram_tensor("mod_dram", [1, 6 * D], F32).ap()
        g_dram = nc.dram_tensor("g_dram", [NGRP, P, 32, P], F32).ap()

        consts_in = sem("consts_in")
        x_in = sem("x_in")
        stage_in = [sem("stage_in0"), sem("stage_in1")]
        mod_stored = sem("mod_stored")
        par_in = sem("par_in")
        x2_in = sem("x2_in")
        keys_in = sem("keys_in")
        g_stored = [sem("g_stored0"), sem("g_stored1")]
        g_in = sem("g_in")
        out_stored = sem("out_stored")
        zeroed = sem("zeroed")
        ident_ready = sem("ident_ready")
        tanh_c = sem("tanh_c")
        crep_ready = sem("crep_ready")
        mask_ready = sem("mask_ready")
        mod_ready = sem("mod_ready")
        var_ready = sem("var_ready")
        std_ready = sem("std_ready")
        norm_ready = sem("norm_ready")
        hT_ready = sem("hT_ready")
        hi_done = sem("hi_done")
        lo_done = sem("lo_done")
        tile_ready = sem("tile_ready")
        tile_free = sem("tile_free")
        aux_ready = sem("aux_ready")
        aux_free = sem("aux_free")
        act_ready = sem("act_ready")
        ev_free = sem("ev_free")
        x1_ready = sem("x1_ready")
        sc_ready = sem("sc_ready")
        sc_free = sem("sc_free")
        sc_used = sem("sc_used")
        s_shift = sem("s_shift")
        s_exp = sem("s_exp")
        gate_ready = sem("gate_ready")
        oh_ready = sem("oh_ready")
        g_ready = sem("g_ready")
        g_free = sem("g_free")
        a_free = sem("a_free")
        g_used = sem("g_used")
        c_ready = sem("c_ready")
        v_ready = sem("v_ready")
        v_free = sem("v_free")
        y_ready = sem("y_ready")
        dve_step = sem("dve_step")

        block = ctx.enter_context(nc.Block())

        def wait(eng, s, value):
            if not isinstance(value, int) or value > 0:
                eng.wait_ge(s, value)

        def front_units(rows):
            return w_front[rows].rearrange("p k n -> p (k n)")

        @block.sync
        def _(sp):
            sp.dma_start(ccol[:, :], c_col).then_inc(consts_in, 16)
            sp.dma_start(cw[:, :, :], conv_w).then_inc(consts_in, 16)
            sp.dma_start(mod, b_cond.partition_broadcast(P)).then_inc(consts_in, 16)
            for u in range(2):
                sp.dma_start(stage[:, u, :], w_cond[u]).then_inc(stage_in[u], 16)
            sp.dma_start(xt, x.rearrange("(b p) d -> p b d", p=P)).then_inc(x_in, 16)
            sp.dma_start(par[:, 0, :], ln_g.partition_broadcast(P)).then_inc(consts_in, 16)
            sp.dma_start(par[:, 1, :], ln_b.partition_broadcast(P)).then_inc(consts_in, 16)
            sp.dma_start(ws_t, w_spat).then_inc(consts_in, 16)
            sp.dma_start(bs_b[:, :, :].rearrange("p g i -> p (g i)"), b_spat.partition_broadcast(P)).then_inc(consts_in, 16)
            with sp.Fori(1, NCOND // 2) as i:
                for u in range(2):
                    sp.wait_ge(aux_ready, i * 2 + (u - 1))
                    sp.dma_start(stage[:, u, :], w_cond[i * 2 + u]).then_inc(stage_in[u], 16)
            for u in range(2):
                sp.wait_ge(aux_ready, NCOND - 1 + u)
                sp.dma_start(stage[:, u, :], front_units(u)).then_inc(stage_in[u], 16)
            sp.wait_ge(mod_ready, 1)
            sp.dma_start(mod_dram, mod[0:1, :]).then_inc(mod_stored, 16)

            def load_pairs(first, last):
                with sp.Fori(first // 2, last // 2) as i:
                    for u in range(2):
                        sp.wait_ge(lo_done, i * 2 + (u - 1))
                        sp.dma_start(stage[:, u, :], front_units(i * 2 + u)).then_inc(stage_in[u], 16)

            load_pairs(2, U_O + N_O)
            sp.wait_ge(tile_ready, T_O)
            sp.wait_ge(mod_stored, 16)
            sp.dma_start(x2, x.rearrange("(b p) d -> p b d", p=P)).then_inc(x2_in, 16)
            sp.dma_start(par[:, 0, :], mod_dram[0, 2 * D:3 * D].partition_broadcast(P)).then_inc(par_in, 16)
            sp.dma_start(par[:, 1, :], ln1_g.partition_broadcast(P)).then_inc(par_in, 16)
            sp.dma_start(par[:, 2, :], ln1_b.partition_broadcast(P)).then_inc(par_in, 16)
            sp.wait_ge(ev_free, E_END)
            sp.dma_start(sh2b, mod_dram[0, 3 * D:4 * D].partition_broadcast(P)).then_inc(par_in, 16)
            sp.dma_start(sc2b, mod_dram[0, 4 * D:5 * D].partition_broadcast(P)).then_inc(par_in, 16)
            load_pairs(U_Q, U_Q + 2)
            sp.wait_ge(x1_ready, 1)
            sp.dma_start(keys_sb, keys_t).then_inc(keys_in, 16)
            load_pairs(U_Q + 2, U_PEER)

            def load_u(n, g, half):
                sp.wait_ge(lo_done, n - 1)
                sp.dma_start(stage[:, half, :], u_units[g * 2 + half]).then_inc(stage_in[half], 16)

            def load_v(n, g, half):
                sp.wait_ge(lo_done, n - 1)
                sp.dma_start(stage[:, half, :].rearrange("p (j d) -> p j d", j=4),
                             expert_v[g][:, :, half * HT:half * HT + HT]).then_inc(stage_in[half], 16)

            for half in range(2):
                load_u(U_PEER + half, 0, half)
            for half in range(2):
                load_u(U_PEER + 2 + half, 1, half)
            sp.wait_ge(sc_ready, 4 * HEADS)
            sp.dma_start(par[:, 0, :], mod_dram[0, 5 * D:6 * D].partition_broadcast(P)).then_inc(par_in, 16)
            sp.dma_start(par[:, 1, :], ln2_g.partition_broadcast(P)).then_inc(par_in, 16)
            sp.dma_start(par[:, 2, :], ln2_b.partition_broadcast(P)).then_inc(par_in, 16)
            with sp.Fori(0, 16) as i:
                for b in range(2):
                    sp.wait_ge(g_free, i * 16 + 8 * (b + 1))
                    sp.dma_start(g_dram[:, :, i * 2 + b, :].rearrange("g p n -> p g n"),
                                 gbuf[b].rearrange("p (g j) t -> p g (j t)", g=NGRP)).then_inc(g_stored[b], 16)
            for b in range(2):
                sp.wait_ge(g_stored[b], 16 * 16)
            sp.dma_start(G_t, g_dram[0].rearrange("p n (j t) -> p n j t", j=4)).then_inc(g_in, 16)

            def load_group(i):
                for half in range(2):
                    load_v(i * 4 + (U_PEER + 4 + half), i, half)
                sp.wait_ge(g_used, i + 1)
                sp.dma_start(G_t, g_dram[i + 1].rearrange("p n (j t) -> p n j t", j=4)).then_inc(g_in, 16)

            with sp.Fori(0, NGRP - 2) as i:
                load_group(i)
                for half in range(2):
                    load_u(i * 4 + (U_PEER + 6 + half), i + 2, half)
            load_group(NGRP - 2)
            for half in range(2):
                load_v(U_PEER + 4 * NGRP - 2 + half, NGRP - 1, half)
            for b in range(NB):
                sp.wait_ge(y_ready, b + 1)
                sp.dma_start(out[b * P:(b + 1) * P, :], xt[:, b, :]).then_inc(out_stored, 16)
            sp.wait_ge(out_stored, 16 * NB)

        @block.gpsimd
        def _(pool):
            pool.memset(ident[:, :], 0.0).then_inc(zeroed, 1)
            pool.wait_ge(zeroed, 1)
            pool.affine_select(out=ident[:, :], in_=ident[:, :], compare_op=ALU.not_equal, fill=1.0, base=0,
                               pattern=[[-1, P]], channel_multiplier=1).then_inc(ident_ready, 1)
            pool.iota(iota_i[:, :], pattern=[[1, P]], base=0, channel_multiplier=0).then_inc(ident_ready, 1)
            pool.wait_ge(consts_in, 16 * 7)
            pool.wait_ge(ident_ready, 2)
            pool.memset(ws_t[64:P, :, 0:64], 0.0).then_inc(mask_ready, 1)

        @block.scalar
        def _(act):
            def make_hi(n, p, pair):
                act.wait_ge(stage_in[p], pair * 16 + 16 * (NCOND // 2 + 1))
                nc.scalar.activation(w_hi[:, p, :], stage[:, p, :], ACT.Copy, scale=WS).then_inc(hi_done, 1)

            def evacuate(t, dst, src, func=ACT.Copy, scale=DESCALE):
                act.wait_ge(tile_ready, t + 1)
                nc.scalar.activation(dst, src, func, scale=scale).then_inc(tile_free, 1)

            def root(k):
                act.wait_ge(var_ready, k + 1)
                nc.scalar.activation(std[:, :], vare[:, :], ACT.Sqrt).then_inc(std_ready, 1)

            def feature_unit(t, dst, func=ACT.Copy, scale=DESCALE):
                for j in range(2):
                    for half in range(2):
                        evacuate(t + 2 * j + half, dst[:, j, half * HT:(half + 1) * HT],
                                 psU[2 * j + half][:, :], func, scale)

            act.wait_ge(consts_in, 16 * 7)
            nc.scalar.activation(cth[:, :], ccol[:, :], ACT.Tanh, scale=0.5).then_inc(tanh_c, 1)
            root(0)
            for p in range(2):
                make_hi(p, p, 0)
            for u in range(N_V):
                for b in range(NB):
                    evacuate(T_V + 8 * u + b, xt[:, b, u * UC:(u + 1) * UC], psU[b % 4][:, 0:UC], ACT.Gelu_apprx_tanh)
                make_hi(u + 2, u % 2, (u + 2) // 2)
            root(1)
            with act.Fori(0, 2) as i:
                for q in range(2):
                    for r, dst in enumerate((evAd, evB, evB)):
                        m = 3 * q + r
                        wait(act, ev_free, i * 4 + (E_CONV + 2 * q + r // 2))
                        feature_unit(i * 24 + (T_CONV + 4 * m), dst)
                        make_hi(None, m % 2, i * 3 + (U_CONV + m + 2) // 2)
            for j in range(N_U):
                act.wait_ge(ev_free, E_U + max(0, j - 1))
                feature_unit(T_U + 4 * j, (evAd, evB)[j % 2], ACT.Gelu_apprx_tanh)
                make_hi(None, j % 2, (U_U + j + 2) // 2)
            with act.Fori(0, 4) as i:
                for r, dst in enumerate((evAd, evB, evC, evB)):
                    act.wait_ge(ev_free, i * 2 + (E_MERGE + r // 3))
                    if r % 2:
                        feature_unit(i * 16 + (T_MERGE + 4 * r), dst, ACT.Tanh, 0.5 * DESCALE)
                    else:
                        feature_unit(i * 16 + (T_MERGE + 4 * r), dst)
                    make_hi(None, r % 2, i * 2 + (U_MERGE + r + 2) // 2)
            for u in range(N_O):
                for b in range(NB):
                    evacuate(T_O + 8 * u + b, xt[:, b, u * UC:(u + 1) * UC], psU[b % 4][:, 0:UC])
                make_hi(None, u % 2, (U_O + u + 2) // 2)
            root(2)
            root(3)
            for h in range(HEADS):
                wait(act, sc_ready, 4 * (h - 1))
                feature_unit(T_Q + 4 * h, qb[h % 2])
                make_hi(None, h % 2, (U_Q + h + 2) // 2)
                wait(act, sc_used, h - 1)
                for t in range(4):
                    act.wait_ge(sc_ready, 4 * h + t + 1)
                    nc.scalar.activation(sc[h % 2][:, 2 * t:2 * t + 2, :, :].rearrange("p b h k -> p (b h k)"),
                                         psX[t][:, :], ACT.Copy).then_inc(sc_free, 1)
            act.wait_ge(s_shift, 1)
            s_flat = s_all.rearrange("p b h k -> p (b h k)")
            nc.scalar.activation(s_flat, s_flat, ACT.Exp).then_inc(s_exp, 1)

            def collect(i):
                for b in range(2):
                    wait(act, g_stored[b], i * 16)
                    for q in range(8):
                        act.wait_ge(g_ready, i * 16 + (8 * b + q + 1))
                        nc.scalar.activation(gbuf[b][:, :, 4 * q:4 * q + 4],
                                             psX[q % 4][:, :].rearrange("p (t k) -> p k t", t=4),
                                             ACT.Copy, scale=1.0 / GS).then_inc(g_free, 1)

            collect(0)
            with act.Fori(1, 16) as i:
                collect(i)

            def expert_acts(t, i, first, hi_pair):
                for half in range(2):
                    if half == 0 and not first:
                        act.wait_ge(a_free, i + 1)
                    feature_unit(t + 4 * half, A_t[:, 2 * half:2 * half + 2, :], ACT.Gelu_apprx_tanh)
                    make_hi(None, half, hi_pair)

            for b in range(2):
                act.wait_ge(g_stored[b], 16 * 16)
            expert_acts(T_PEER, 0, True, (U_PEER + 2) // 2)
            with act.Fori(0, NGRP - 1) as i:
                expert_acts(i * 8 + (T_PEER + 8), i, False, i * 2 + (U_PEER + 4) // 2)
                for half in range(2):
                    act.wait_ge(v_ready, i * 16 + 8 * (half + 1))
                    make_hi(None, half, i * 2 + (U_PEER + 6) // 2)
            root(4)

        @block.vector
        def _(dve):
            V = nc.vector
            count = [0]
            base = [0]

            def step(ins):
                count[0] += 1
                return ins.then_inc(dve_step, 1)

            def settle():
                dve.wait_ge(dve_step, base[0] + count[0])

            def in_loop(i, iterations, body):
                start, outer = count[0], base[0]
                per = steps_of[body]
                base[0] = i * per + start
                count[0] = 0
                body(i)
                assert count[0] == per, (body, count[0])
                base[0] = outer
                count[0] = start + per * iterations

            def make_lo(n, p):
                dve.wait_ge(hi_done, n + 1)
                V.scalar_tensor_tensor(w_lo[:, p, :], stage[:, p, :], WS, w_hi[:, p, :],
                                       ALU.mult, ALU.subtract).then_inc(lo_done, 1)

            def split(hi, lo, src, scale, done):
                step(V.tensor_scalar(hi, src, scale, None, ALU.mult))
                settle()
                V.scalar_tensor_tensor(lo, src, scale, hi, ALU.mult, ALU.subtract).then_inc(done, 1)

            def statistics(src):
                for b in range(NB):
                    for half in range(2):
                        step(V.bn_stats(stats[:, b, half, :], src[:, b, half * HT:(half + 1) * HT]))
                settle()
                for b in range(NB):
                    step(V.bn_aggr(mv[:, b, :], stats[:, b, :, :]))
                settle()
                V.tensor_scalar(vare[:, :], mv[:, :, 1], EPS, None, ALU.add).then_inc(var_ready, 1)

            def normalise(k, dst, src):
                dve.wait_ge(std_ready, k + 1)
                step(V.reciprocal(rstd[:, :], std[:, :]))
                settle()
                for b in range(NB):
                    step(V.tensor_scalar(dst[:, b, :], src[:, b, :], mv[:, b, 0:1], rstd[:, b:b + 1],
                                         ALU.subtract, ALU.mult))
                settle()

            def row(ap):
                return ap.unsqueeze(1).to_broadcast([P, NB, D])

            def affine(dst, gain, bias, done):
                step(V.tensor_tensor(dst, dst, row(gain), ALU.mult))
                settle()
                V.tensor_tensor(dst, dst, row(bias), ALU.add).then_inc(done, 1)

            def split_transposed(first):
                for k in range(KD):
                    for half in range(2):
                        a = 2 * k + half
                        dve.wait_ge(aux_ready, first + a + 1)
                        hi, lo = (h[:, k, half * HT:(half + 1) * HT] for h in (h_hi, h_lo))
                        step(V.tensor_scalar(hi, psX[a % 4][:, :], AS, None, ALU.mult))
                        settle()
                        V.scalar_tensor_tensor(lo, psX[a % 4][:, :], AS, hi, ALU.mult,
                                               ALU.subtract).then_inc(aux_free, 1)

            dve.wait_ge(ident_ready, 2)
            step(V.tensor_copy(iota16b[:, :], iota_i[:, :]))
            step(V.tensor_copy(iota_f[:, :], iota_i[:, 0:TOPK]))
            V.memset(evA[:, :, 0:2], 0.0).then_inc(ev_free, 1)
            dve.wait_ge(tanh_c, 1)
            step(V.tensor_scalar(cth[:, :], cth[:, :], 1.0, 0.5, ALU.add, ALU.mult))
            settle()
            step(V.tensor_tensor(cth[:, :], cth[:, :], ccol[:, :], ALU.mult))
            settle()
            V.tensor_copy(crep, cth[:, :].unsqueeze(2).to_broadcast([P, KD, P])).then_inc(crep_ready, 1)
            dve.wait_ge(x_in, 16)
            statistics(xt)
            normalise(0, xt, xt)
            for u in range(NCOND):
                dve.wait_ge(aux_ready, u + 1)
                cols = mod[:, u * UC:(u + 1) * UC]
                V.tensor_tensor(cols, psX[u % 4][:, 0:UC], cols, ALU.add).then_inc(aux_free, 1)
            dve.wait_ge(aux_free, NCOND)
            step(V.tensor_scalar(mod[:, D:2 * D], mod[:, D:2 * D], 1.0, None, ALU.add))
            V.tensor_scalar(mod[:, 4 * D:5 * D], mod[:, 4 * D:5 * D], 1.0, None, ALU.add).then_inc(mod_ready, 1)
            settle()
            affine(xt, mod[:, D:2 * D], mod[:, 0:D], norm_ready)
            split_transposed(A_HT)
            make_lo(0, 0)
            make_lo(1, 1)
            for u in range(N_V):
                dve.wait_ge(tile_free, T_V + 8 * (u + 1))
                make_lo(u + 2, u % 2)
            statistics(xt)
            normalise(1, xt, xt)
            affine(xt, par[:, 0, :], par[:, 1, :], norm_ready)

            def conv(i):
                for q in range(2):
                    qc = i * 4 + 2 * q
                    m = 3 * q
                    t = i * 24 + (T_CONV + 4 * m)
                    n = i * 6 + (U_CONV + m + 2)
                    make_lo(n, m % 2)
                    make_lo(n + 1, (m + 1) % 2)
                    dve.wait_ge(tile_free, t + 8)
                    V.tensor_tensor(evAd, evAd, evB, ALU.mult).then_inc(ev_free, 1)
                    dve.wait_ge(ev_free, i * 4 + (E_CONV + 2 * q + 1))
                    for j in range(2):
                        step(V.tensor_scalar(evC[:, j, :], evA[:, j, 0:S], cw[:, bass.ds(qc + j, 1), 0:1].rearrange("p a b -> p (a b)"),
                                             None, ALU.mult))
                    settle()
                    for tap in (1, 2):
                        for j in range(2):
                            step(V.scalar_tensor_tensor(evC[:, j, :], evA[:, j, tap:tap + S],
                                                        cw[:, bass.ds(qc + j, 1), tap:tap + 1].rearrange("p a b -> p (a b)"),
                                                        evC[:, j, :], ALU.mult, ALU.add))
                        settle()
                    make_lo(n + 2, m % 2)
                    dve.wait_ge(tile_free, t + 12)
                    step(V.tensor_tensor(evC, evC, evB, ALU.mult))
                    settle()
                    step(V.tensor_scalar(yb_hi[:, bass.ds(qc, 2), :], evC, AS, None, ALU.mult))
                    settle()
                    V.scalar_tensor_tensor(yb_lo[:, bass.ds(qc, 2), :], evC, AS, yb_hi[:, bass.ds(qc, 2), :],
                                           ALU.mult, ALU.subtract).then_inc(ev_free, 1)

            def merge(i):
                qc = i * 2
                t = i * 16 + T_MERGE
                n = i * 4 + (U_MERGE + 2)
                make_lo(n, 0)
                make_lo(n + 1, 1)
                dve.wait_ge(tile_free, t + 8)
                V.scalar_tensor_tensor(evAd, evB, 1.0, evAd, ALU.add, ALU.mult).then_inc(ev_free, 1)
                make_lo(n + 2, 0)
                make_lo(n + 3, 1)
                dve.wait_ge(tile_free, t + 16)
                step(V.scalar_tensor_tensor(evC, evB, 1.0, evC, ALU.add, ALU.mult))
                settle()
                dve.wait_ge(ev_free, i * 2 + (E_MERGE + 1))
                step(V.tensor_tensor(evAd, evAd, evC, ALU.add))
                settle()
                step(V.tensor_scalar(m_hi[:, bass.ds(qc, 2), :], evAd, 0.5 * AS, None, ALU.mult))
                settle()
                V.scalar_tensor_tensor(m_lo[:, bass.ds(qc, 2), :], evAd, 0.5 * AS, m_hi[:, bass.ds(qc, 2), :],
                                       ALU.mult, ALU.subtract).then_inc(ev_free, 1)

            def coefficients(i):
                dve.wait_ge(tile_free, i * 8 + (T_PEER + 8))
                dve.wait_ge(g_in, i * 16 + 16)
                for j in range(4):
                    a = A_t[:, j, :].rearrange("p (n t) -> p n t", n=32)
                    ins = V.scalar_tensor_tensor(a, a, AS, G_t[:, :, j, :], ALU.mult, ALU.mult)
                    if j < 3:
                        step(ins)
                ins.then_inc(g_used, 1)
                dve.wait_ge(g_used, i + 1)
                step(V.tensor_scalar(c_hi, A_t, 1.0, None, ALU.mult))
                settle()
                V.tensor_tensor(c_lo, A_t, c_hi, ALU.subtract).then_inc(a_free, 1)

            def gather_out(i):
                for half in range(2):
                    for b in range(NB):
                        dve.wait_ge(v_ready, i * 16 + (8 * half + b + 1))
                        dst = acc[:, b, half * HT:(half + 1) * HT]
                        V.tensor_tensor(dst, psX[b % 4][:, :], dst, ALU.add).then_inc(v_free, 1)
                    yield half

            def experts(i):
                n = i * 4 + (U_PEER + 4)
                coefficients(i)
                make_lo(n, 0)
                make_lo(n + 1, 1)
                for half in gather_out(i):
                    make_lo(n + 2 + half, half)

            def onehots(i):
                for q in range(16):
                    wait(dve, g_ready, i * 16 + (q - 3))
                    for t in range(4):
                        def col(a):
                            return a[:, bass.ds(i * 64 + (4 * q + t), 1)]
                        V.tensor_scalar(oh[:, q % 4, t, 0, :], iota16b[:, :], col(i1_t), None, ALU.is_equal)
                        V.tensor_scalar(oh[:, q % 4, t, 1, :], iota16b[:, :], col(i2_t), col(g_t),
                                        ALU.is_equal, ALU.mult)
                        ins = V.tensor_scalar(oh[:, q % 4, t, 2, :], iota16b[:, :], col(i2_t), col(glo_t),
                                              ALU.is_equal, ALU.mult)
                    ins.then_inc(oh_ready, 1)

            steps_of = {conv: 16, merge: 3, experts: 4}

            with dve.Fori(0, 2) as i:
                in_loop(i, 2, conv)
            for a in range(16):
                g, half = a // 2, a % 2
                dve.wait_ge(aux_ready, A_MIX + a + 1)
                V.tensor_tensor(mixb[:, g, half * HT:(half + 1) * HT].rearrange("p (n i) -> p n i", n=4),
                                psX[a % 4][:, :].rearrange("p (n i) -> p n i", n=4),
                                bs_b[:, g:g + 1, :].to_broadcast([P, 4, P]), ALU.add).then_inc(aux_free, 1)
            dve.wait_ge(aux_free, A_H2T)
            for j in range(N_U):
                make_lo(U_U + j + 2, j % 2)
                dve.wait_ge(tile_free, T_U + 4 * (j + 1))
                ev = (evAd, evB)[j % 2]
                step(V.tensor_tensor(ev, ev, mixb[:, 2 * j:2 * j + 2, :], ALU.mult))
                settle()
                split(ya_hi[:, 2 * j:2 * j + 2, :], ya_lo[:, 2 * j:2 * j + 2, :], ev, AS, ev_free)
            with dve.Fori(0, 4) as i:
                in_loop(i, 4, merge)
            for u in range(N_O):
                make_lo(U_O + u + 2, u % 2)
            dve.wait_ge(tile_free, T_Q)
            dve.wait_ge(par_in, 16 * 5)
            dve.wait_ge(x2_in, 16)
            step(V.tensor_tensor(xt, xt, row(par[:, 0, :]), ALU.mult))
            settle()
            step(V.scalar_tensor_tensor(R1[:, :], R2[:, :], ALPHA, R1[:, :], ALU.mult, ALU.add))
            settle()
            statistics(xt)
            normalise(2, xt, xt)
            affine(xt, par[:, 1, :], par[:, 2, :], x1_ready)
            dve.wait_ge(x1_ready, 1)
            statistics(xt)
            normalise(3, x2, xt)
            affine(x2, sc2b, sh2b, norm_ready)
            split_transposed(A_H2T)

            def best16(values, places, pool_of, spare, n):
                def at(i):
                    return values(i), places(i), pool_of(i), spare(i)
                for i in range(n):
                    v, p, src, s = at(i)
                    step(V.max(v[:, 0:8], src))
                settle()
                for i in range(n):
                    v, p, src, s = at(i)
                    step(V.max_index(p[:, 0:8], v[:, 0:8], src))
                    step(V.match_replace(s, v[:, 0:8], src, LOWEST))
                settle()
                for i in range(n):
                    v, p, src, s = at(i)
                    step(V.max(v[:, 8:16], s))
                settle()
                for i in range(n):
                    v, p, src, s = at(i)
                    step(V.max_index(p[:, 8:16], v[:, 8:16], s))
                settle()

            for h in range(HEADS):
                s = sc[h % 2]
                dve.wait_ge(tile_free, T_Q + 4 * (h + 1))
                make_lo(U_Q + h + 2, h % 2)
                dve.wait_ge(sc_free, 4 * (h + 1))
                best16(lambda i: vals[:, i // 2, i % 2, :], lambda i: idx[:, i // 2, i % 2, :],
                       lambda i: s[:, i // 2, i % 2, :], lambda i: sc2[:, i // 2, i % 2, :], 2 * NB)
                V.tensor_copy(idxf, idx).then_inc(sc_used, 1)
                step(V.tensor_tensor(cand, vals[:, :, 0, :].unsqueeze(3).to_broadcast([P, NB, TOPK, TOPK]),
                                     vals[:, :, 1, :].unsqueeze(2).to_broadcast([P, NB, TOPK, TOPK]), ALU.add))
                settle()
                best16(lambda i: tops[:, i, :], lambda i: sel[:, i, :],
                       lambda i: cand[:, i, :, :].rearrange("p i j -> p (i j)"), lambda i: cand2[:, i, :], NB)
                step(V.tensor_copy(s_all[:, :, h, :], tops))
                sel_flat = sel.rearrange("p b k -> p (b k)")
                step(V.tensor_scalar(sel_a, sel_flat, 4, None, ALU.logical_shift_right))
                step(V.tensor_scalar(sel_b, sel_flat, 15, None, ALU.bitwise_and))
                settle()
                step(V.tensor_copy(sel_af, sel_a))
                step(V.tensor_copy(sel_bf, sel_b))
                settle()
                dve.wait_ge(sc_used, h + 1)
                for half, place, dst in ((0, sel_af, i1_all), (1, sel_bf, i2_all)):
                    step(V.tensor_tensor(cmp_t, place.unsqueeze(2).to_broadcast([P, NB * TOPK, TOPK]),
                                         iota_f[:, :].unsqueeze(1).to_broadcast([P, NB * TOPK, TOPK]), ALU.is_equal))
                    settle()
                    by_block = cmp_t.rearrange("p (b k) j -> p b k j", b=NB)
                    step(V.tensor_tensor(by_block, by_block,
                                         idxf[:, :, half, :].unsqueeze(2).to_broadcast([P, NB, TOPK, TOPK]), ALU.mult))
                    settle()
                    step(V.tensor_reduce(dst[:, :, h, :], by_block, AX_X, ALU.add))
                    settle()
            s3 = s_all.rearrange("p b h k -> p (b h) k")
            rows3 = [P, NB * HEADS, TOPK]
            step(V.tensor_copy(rsum, s3[:, :, 0]))
            settle()
            V.tensor_tensor(s3, s3, rsum.unsqueeze(2).to_broadcast(rows3), ALU.subtract).then_inc(s_shift, 1)
            dve.wait_ge(s_exp, 1)
            step(V.tensor_reduce(rsum, s3, AX_X, ALU.add))
            settle()
            step(V.reciprocal(rinv, rsum))
            settle()
            V.tensor_tensor(s3, s3, rinv.unsqueeze(2).to_broadcast(rows3), ALU.mult).then_inc(gate_ready, 1)
            for a in range(6):
                kind, half = a // 2, a % 2
                cols = slice(half * HT, (half + 1) * HT)
                dve.wait_ge(aux_ready, A_IDX + a + 1)
                if kind < 2:
                    V.tensor_copy((i1_t, i2_t)[kind][:, cols], psX[a % 4][:, :]).then_inc(aux_free, 1)
                else:
                    V.tensor_scalar(g_t[:, cols], psX[a % 4][:, :], GS, None, ALU.mult).then_inc(aux_free, 1)
            dve.wait_ge(aux_free, A_END)
            step(V.tensor_copy(g16, g_t))
            settle()
            step(V.tensor_tensor(glo_t, g_t, g16, ALU.subtract))
            settle()
            onehots(0)
            with dve.Fori(1, 16) as i:
                onehots(i)
            dve.wait_ge(g_ready, 256)
            step(V.memset(R3[:, 4096:4096 + 8192], 0.0))
            settle()
            make_lo(U_PEER + 2, 0)
            make_lo(U_PEER + 3, 1)
            with dve.Fori(0, NGRP - 1) as i:
                in_loop(i, NGRP - 1, experts)
            coefficients(NGRP - 1)
            for half in gather_out(NGRP - 1):
                pass
            dve.wait_ge(v_free, 16 * NGRP)
            dve.wait_ge(par_in, 16 * 8)
            step(V.scalar_tensor_tensor(acc, acc, DESCALE, row(par[:, 0, :]), ALU.mult, ALU.mult))
            settle()
            step(V.scalar_tensor_tensor(xt, xt, ALPHA, acc, ALU.mult, ALU.add))
            settle()
            statistics(xt)
            normalise(4, xt, xt)
            for b in range(NB):
                step(V.tensor_tensor(xt[:, b, :], xt[:, b, :], par[:, 1, :], ALU.mult))
            settle()
            for b in range(NB):
                V.tensor_tensor(xt[:, b, :], xt[:, b, :], par[:, 2, :], ALU.add).then_inc(y_ready, 1)

        @block.tensor
        def _(pe):
            mm = nc.tensor.matmul

            def aux_tile(a):
                wait(pe, aux_free, a - 3)
                return psX[a % 4]

            def product(ps, lhs, rhs, chunks):
                n = len(chunks)
                for s, k in enumerate(chunks):
                    mm(ps, lhs[0](k), rhs[0](k), start=(s == 0), stop=False)
                    mm(ps, lhs[0](k), rhs[1](k), start=False, stop=False)
                    last = mm(ps, lhs[1](k), rhs[0](k), start=False, stop=(s == n - 1))
                return last

            def w_unit(p, columns):
                return [w[:, p, :].rearrange("p (k n) -> p k n", n=columns) for w in (w_hi, w_lo)]

            def feature_unit(n, p, t, hi, lo):
                pe.wait_ge(lo_done, n + 1)
                w = w_unit(p, UC)
                for j in range(2):
                    for half in range(2):
                        r = 2 * j + half
                        wait(pe, tile_free, t + (r - 3))
                        product(psU[r][:, :],
                                [lambda k, s=s: w[s][:, k, j * P:(j + 1) * P] for s in range(2)],
                                [lambda k, s=s: (hi, lo)[s][:, k, half * HT:(half + 1) * HT] for s in range(2)],
                                range(KD)).then_inc(tile_ready, 1)

            def token_unit(n, p, t, hi, lo):
                pe.wait_ge(lo_done, n + 1)
                w = w_unit(p, UC)
                for b in range(NB):
                    wait(pe, tile_free, t + (b - 3))
                    product(psU[b % 4][:, 0:UC],
                            [lambda k, s=s: (hi, lo)[s][:, k, b * P:(b + 1) * P] for s in range(2)],
                            [lambda k, s=s: w[s][:, k, :] for s in range(2)],
                            range(KD)).then_inc(tile_ready, 1)

            def transposes(first, src):
                for k in range(KD):
                    for half in range(2):
                        ps = aux_tile(first + 2 * k + half)
                        for b in range(4):
                            ins = nc.tensor.transpose(ps[:, b * P:(b + 1) * P], src[:, 4 * half + b, k * P:(k + 1) * P],
                                                      ident[:, :])
                        ins.then_inc(aux_ready, 1)

            pe.wait_ge(crep_ready, 1)
            for u in range(NCOND):
                pe.wait_ge(stage_in[u % 2], 16 * (u // 2 + 1))
                ps = aux_tile(A_COND + u)
                w = stage[:, u % 2, :].rearrange("p (k n) -> p k n", k=KD)
                for k in range(KD):
                    ins = mm(ps[:, 0:UC], crep[:, k, :], w[:, k, :], start=(k == 0), stop=(k == KD - 1))
                ins.then_inc(aux_ready, 1)
            pe.wait_ge(ident_ready, 2)
            pe.wait_ge(norm_ready, 1)
            transposes(A_HT, xt)
            pe.wait_ge(aux_free, A_MIX)
            for u in range(N_V):
                token_unit(U_V + u, u % 2, T_V + 8 * u, h_hi, h_lo)
            with pe.Fori(0, N_CONV // 2) as i:
                for p in range(2):
                    feature_unit(i * 2 + (U_CONV + p), p, i * 8 + (T_CONV + 4 * p), h_hi, h_lo)
            pe.wait_ge(norm_ready, 2)
            pe.wait_ge(mask_ready, 1)
            for a in range(16):
                g, half = a // 2, a % 2
                ps = aux_tile(A_MIX + a)
                for b in range(4):
                    ins = mm(ps[:, b * P:(b + 1) * P], xt[:, 4 * half + b, g * P:(g + 1) * P], ws_t[:, g, :],
                             start=True, stop=True)
                ins.then_inc(aux_ready, 1)
            with pe.Fori(0, N_U // 2) as i:
                for p in range(2):
                    feature_unit(i * 2 + (U_U + p), p, i * 8 + (T_U + 4 * p), h_hi, h_lo)
            pe.wait_ge(ev_free, E_MERGE)
            with pe.Fori(0, 4) as i:
                for r, (hi, lo) in enumerate(((ya_hi, ya_lo), (h_hi, h_lo), (yb_hi, yb_lo), (h_hi, h_lo))):
                    feature_unit(i * 4 + (U_MERGE + r), r % 2, i * 16 + (T_MERGE + 4 * r), hi, lo)
            pe.wait_ge(ev_free, E_END)
            for u in range(N_O):
                token_unit(U_O + u, u % 2, T_O + 8 * u, m_hi, m_lo)
            pe.wait_ge(norm_ready, 3)
            transposes(A_H2T, x2)
            pe.wait_ge(aux_free, A_IDX)
            pe.wait_ge(keys_in, 16)
            for h in range(HEADS):
                feature_unit(U_Q + h, h % 2, T_Q + 4 * h, h_hi, h_lo)
                pe.wait_ge(tile_free, T_Q + 4 * (h + 1))
                for t in range(4):
                    wait(pe, sc_free, 4 * (h - 1) + t + 1)
                    for m in range(4):
                        b, half = 2 * t + m // 2, m % 2
                        ins = mm(psX[t][:, m * P:(m + 1) * P], qb[h % 2][:, half, b * P:(b + 1) * P],
                                 keys_sb[:, 2 * h + half, :], start=True, stop=True)
                    ins.then_inc(sc_ready, 1)
            pe.wait_ge(gate_ready, 1)
            pe.wait_ge(sc_free, 4 * HEADS)
            for a in range(6):
                kind, half = a // 2, a % 2
                ps = aux_tile(A_IDX + a)
                src = (i1_all, i2_all, s_all)[kind].rearrange("p b h k -> p b (h k)")
                for b in range(4):
                    ins = nc.tensor.transpose(ps[:, b * P:(b + 1) * P], src[:, 4 * half + b, :], ident[:, :])
                ins.then_inc(aux_ready, 1)
            pe.wait_ge(aux_free, A_END)

            def spread(i, first):
                for q in range(4):
                    if not first:
                        pe.wait_ge(g_free, i * 4 + (q - 3))
                    pe.wait_ge(oh_ready, i * 4 + (q + 1))
                    for t in range(4):
                        mm(psX[q][:, t * P:(t + 1) * P], oh[:, q, t, 0, :], oh[:, q, t, 1, :], start=True, stop=False)
                        ins = mm(psX[q][:, t * P:(t + 1) * P], oh[:, q, t, 0, :], oh[:, q, t, 2, :],
                                 start=False, stop=True)
                    ins.then_inc(g_ready, 1)

            spread(0, True)
            with pe.Fori(1, 64) as i:
                spread(i, False)
            pe.wait_ge(g_free, 256)

            def expert_in(i, g):
                for half in range(2):
                    feature_unit(i * 4 + (U_PEER + half), half, g * 8 + (T_PEER + 4 * half), h_hi, h_lo)

            def expert_out(n, i, first=False):
                pe.wait_ge(a_free, i + 1)
                for half in range(2):
                    pe.wait_ge(lo_done, n + half + 1)
                    w = w_unit(half, HT)
                    for b in range(NB):
                        if not (first and half == 0 and b < 4):
                            pe.wait_ge(v_free, i * 16 + (8 * half + b - 3))
                        product(psX[b % 4][:, :],
                                [lambda k, s=s: (c_hi, c_lo)[s][:, k, b * P:(b + 1) * P] for s in range(2)],
                                [lambda k, s=s: w[s][:, k, :] for s in range(2)],
                                range(4)).then_inc(v_ready, 1)

            def feature_pair(n, t):
                for half in range(2):
                    feature_unit(n + half, half, t + 4 * half, h_hi, h_lo)

            feature_pair(U_PEER, T_PEER)
            feature_pair(U_PEER + 2, T_PEER + 8)
            expert_out(U_PEER + 4, 0, True)
            with pe.Fori(1, NGRP - 1) as i:
                feature_pair(i * 4 + (U_PEER + 2), i * 8 + (T_PEER + 8))
                expert_out(i * 4 + (U_PEER + 4), i)
            expert_out(U_PEER + 4 * NGRP - 2, NGRP - 1)


def _unit_columns(w):
    return w.reshape(KD, P, -1, UC).transpose(2, 1, 0, 3)


def kernel(**inputs):
    import concourse.bacc as _bacc
    from concourse.bass_utils import run_bass_kernel_spmd as _run

    a = {k: np.asarray(v) for k, v in inputs.items()}
    w_in = _unit_columns(a["w_in"][0])
    part = {name: w_in[4 * i:4 * i + 4] for i, name in enumerate(("u", "v", "gB", "gC", "z", "ga", "gb"))}
    pa, pb = _unit_columns(a["p_a"][0]), _unit_columns(a["p_b"][0])
    order = list(part["v"])
    for q in range(4):
        order += [part["z"][q], part["gC"][q], part["gB"][q]]
    order += list(part["u"])
    for q in range(4):
        order += [pa[q], part["ga"][q], pb[q], part["gb"][q]]
    order += list(_unit_columns(a["w_o"][0])) + list(_unit_columns(a["w_q_peer"][0]))
    arrays = {
        "x": a["x"][0],
        "c_col": a["c"].reshape(KD, P).T,
        "w_cond": _unit_columns(a["w_cond"][0]).reshape(NCOND, P, 2048),
        "b_cond": a["b_cond"][0],
        "w_front": np.stack(order),
        "ln_g": a["gmlp_ln_g"][0],
        "ln_b": a["gmlp_ln_b"][0],
        "w_spat": a["w_spatial"][0].transpose(2, 0, 1),
        "b_spat": a["b_spatial"][0].reshape(-1),
        "conv_w": a["conv_w"][0].reshape(3, KD, P).transpose(2, 1, 0),
        "ln1_g": a["ln1_g"][0],
        "ln1_b": a["ln1_b"][0],
        "keys_t": a["sub_keys"][0].reshape(2 * HEADS, NKEYS, P).transpose(2, 0, 1),
        "u_units": a["expert_u"][0].reshape(P, NGRP, 2, 2, KD, P).transpose(1, 2, 5, 4, 3, 0).reshape(2 * NGRP, P, 2048),
        "expert_v": a["expert_v"][0],
        "ln2_g": a["ln2_g"][0],
        "ln2_b": a["ln2_b"][0],
    }
    nc = _bacc.Bacc("TRN2", target_bir_lowering=False, num_devices=1)
    arrays = {"in_" + k: np.ascontiguousarray(v) for k, v in arrays.items()}
    args = [nc.dram_tensor(k, v.shape, mybir.dt.from_np(v.dtype), kind="ExternalInput").ap() for k, v in arrays.items()]
    names = [k[3:] for k in arrays]
    args[names.index("expert_v")] = args[names.index("expert_v")].rearrange("(p g j) d -> g p j d", p=P, j=4)
    out = nc.dram_tensor("out", (S, D), F32, kind="ExternalOutput").ap()
    trunk_layer(nc, *args, out)
    r = _run(nc, [arrays], core_ids=[0])
    return r.results[0]["out"].reshape(1, S, D)
```

```python
from contextlib import ExitStack

import numpy as np

import concourse.bass as bass
from concourse import mybir

ALU = mybir.AluOpType
ACT = mybir.ActivationFunctionType
F32 = mybir.dt.float32
F16 = mybir.dt.float16
U32 = mybir.dt.uint32
I32 = mybir.dt.int32
AX_X = mybir.AxisListType.X

P = 128
D = 1024
S = 1024
KD = D // P
NB = S // P
GROUPS = 8
HEADS = 8
NKEYS = 128
TOPK = 16
HT = 512
UC = 256
ALPHA = 2.0 ** 0.25
EPS = 1e-5
WS = 256.0
AS = 16.0
DESCALE = 1.0 / (WS * AS)
GS = 4096.0
LOWEST = -3.0e38

NCOND = 6 * D // UC
N_V, N_CONV, N_U, N_MERGE, N_O = 4, 12, 4, 16, 4
U_V = 0
U_CONV = U_V + N_V
U_U = U_CONV + N_CONV
U_MERGE = U_U + N_U
U_O = U_MERGE + N_MERGE
U_Q = U_O + N_O
NGRP = 32
N_TAIL, N_SPREAD, N_POST = 4, 16, 2
U_TAIL = U_Q + 2 * HEADS
U_SPREAD = U_TAIL + N_TAIL
U_POST = U_SPREAD + N_SPREAD
EARLY = (HEADS + N_TAIL + N_SPREAD + N_POST) // 2
U_VE = U_POST + N_POST
U_LATE = U_VE + 2 * EARLY
T_V = 0
T_CONV = T_V + 8 * N_V
T_U = T_CONV + 4 * N_CONV
T_MERGE = T_U + 4 * N_U
T_O = T_MERGE + 4 * N_MERGE
T_Q = T_O + 8 * N_O
T_TAIL = T_Q + 8 * HEADS
T_SPREAD = T_TAIL + 4 * N_TAIL
T_POST = T_SPREAD + 4 * N_SPREAD
T_LATE = T_POST + 4 * N_POST
U_LAST = U_LATE + 2 + 4 * (NGRP - 1 - EARLY)
COND1 = 2 * D // UC
A_HT = COND1
A_COND2 = A_HT + 16
A_MIX = NCOND + 16
A_H2T = A_MIX + 16
A_IDX = A_H2T + 16
A_END = A_IDX + 6
E_CONV = 1
E_U = E_CONV + 8
E_MERGE = E_U + 4
E_END = E_MERGE + 8


def trunk_layer(nc, x, c_col, w_cond, b_cond, w_front, ln_g, ln_b, w_spat, b_spat, conv_w,
                ln1_g, ln1_b, keys_t, u_units, expert_v, ln2_g, ln2_b, out):
    with ExitStack() as ctx:
        def sb(name, shape, dt=F32):
            return ctx.enter_context(nc.sbuf_tensor(name, shape, dt))

        def sem(name):
            return ctx.enter_context(nc.semaphore(name))

        stage = sb("stage", [P, 2, 2048])
        w_hi = sb("w_hi", [P, 2, 2048], F16)
        w_lo = sb("w_lo", [P, 2, 2048], F16)
        h_hi = sb("h_hi", [P, KD, S], F16)
        h_lo = sb("h_lo", [P, KD, S], F16)
        R1 = sb("R1", [P, 8192])
        R2 = sb("R2", [P, 8192])
        R3 = sb("R3", [P, 8192 + 2052 + 2048 + 2048])
        par = sb("par", [P, 3, D])
        ring = sb("ring", [P, 4, HT])
        ident = sb("ident", [P, P])
        iota_i = sb("iota_i", [P, P], I32)
        iota_f = sb("iota_f", [P, TOPK])
        cw = sb("cw", [P, KD, 3])
        ccol = sb("ccol", [P, KD])
        cth = sb("cth", [P, KD])
        cols = sb("cols", [P, 4, KD])
        stats = sb("stats", [P, NB, 4, 6])
        mv = sb("mv", [P, NB, 2])
        vare = sb("vare", [P, NB])
        std = sb("std", [P, NB])
        rstd = sb("rstd", [P, NB])
        unread = sb("unread", [P, 1])

        def view(region, at, n, dt=F32):
            v = region[:, at:at + n]
            return v.bitcast(dt) if dt != F32 else v

        def v3(ap, a):
            return ap.rearrange("p (a b) -> p a b", a=a)

        xt = v3(view(R1, 0, 8192), NB)
        ya_hi = v3(view(R1, 0, 4096, F16), KD)
        ya_lo = v3(view(R1, 4096, 4096, F16), KD)
        yb_hi = v3(view(R2, 0, 4096, F16), KD)
        yb_lo = v3(view(R2, 4096, 4096, F16), KD)
        x2 = v3(view(R2, 0, 8192), NB)
        mod = view(R3, 0, 6144)
        crep = v3(view(R3, 6144, 1024), KD)
        mixb = v3(view(R3, 0, 8192), GROUPS)
        m_hi = v3(view(R3, 0, 4096, F16), KD)
        m_lo = v3(view(R3, 4096, 4096, F16), KD)
        evA = v3(view(R3, 8192, 2052), 2)
        evB = v3(view(R3, 10244, 2048), 2)
        evC = v3(view(R3, 12292, 2048), 2)
        evAd = evA[:, :, 2:2 + S]
        cond_ring = v3(view(R2, 0, 8192), 4)
        diag = view(R3, 12292, 2048).rearrange("p (a b) -> p a b", b=P)
        bs_b = ring[:, 0:2, :].rearrange("p a (g i) -> p (a g) i", i=P)
        ws_t = v3(par[:, 2, :], GROUPS)
        qb = [v3(view(R2, 2048 * i, 2048), 2) for i in range(2)]
        sc = [view(R2, 4096 + 2048 * i, 2048).rearrange("p (b h k) -> p b h k", b=NB, h=2) for i in range(2)]
        keys_sb = par[:, 0:2, :].rearrange("p a (g k) -> p (a g) k", k=NKEYS)
        sc2 = view(R3, 0, 2048).rearrange("p (b h k) -> p b h k", b=NB, h=2)
        cand = view(R3, 2048, 2048).rearrange("p (b i j) -> p b i j", b=NB, i=TOPK)
        cand2 = v3(view(R3, 4096, 2048), NB)
        cmp_t = v3(view(R3, 6144, 2048), NB * TOPK)
        vals = view(R3, 8192, 256).rearrange("p (b h k) -> p b h k", b=NB, h=2)
        idx = view(R3, 8448, 256, U32).rearrange("p (b h k) -> p b h k", b=NB, h=2)
        idxf = view(R3, 8704, 256).rearrange("p (b h k) -> p b h k", b=NB, h=2)
        sel = v3(view(R3, 8960, 128, U32), NB)
        sel_a = view(R3, 9088, 128, U32)
        sel_b = view(R3, 9216, 128, U32)
        sel_af = view(R3, 9344, 128)
        sel_bf = view(R3, 9472, 128)
        tops = v3(view(R3, 9600, 128), NB)
        rsum = view(R3, 9728, 64)
        rinv = view(R3, 9792, 64)
        i1_all = view(R3, 10244, 1024).rearrange("p (b h k) -> p b h k", b=NB, h=HEADS)
        i2_all = view(R3, 11268, 1024).rearrange("p (b h k) -> p b h k", b=NB, h=HEADS)
        s_all = view(R3, 12292, 1024).rearrange("p (b h k) -> p b h k", b=NB, h=HEADS)
        keys_t16 = v3(view(R3, 0, 1024, F16), 2)
        gates16 = v3(view(R3, 1024, 1024, F16), 2)
        g_t = view(R3, 2048, 1024)
        iota_k4 = v3(view(R3, 3072, 256, F16), P)
        oh_keys = view(R3, 3328, 4 * 512, F16).rearrange("p (r c k t) -> p r c k t", r=4, c=2, t=4)
        oh_gate = view(R3, 5376, 4 * 512, F16).rearrange("p (r c k t) -> p r c k t", r=4, c=2, t=4)
        gbuf = [view(R2, 4096 * i, 4096).rearrange("p (k t) -> p k t", t=32) for i in range(2)]
        A_t = v3(view(R2, 0, 4096), 4)
        G_t = view(R2, 4096, 4096).rearrange("p (n j t) -> p n j t", n=32, j=4)
        c_hi = [v3(view(R3, 0, 2048, F16), 4), v3(view(R3, 12288, 2048, F16), 4)]
        c_lo = [v3(view(R3, 2048, 2048, F16), 4),
                ring[:, :, :].rearrange("p a b -> p (a b)").bitcast(F16).rearrange("p (a b) -> p a b", a=4)]
        acc = v3(view(R3, 4096, 8192), NB)

        psU = [ctx.enter_context(nc.psum_tensor(f"psU{i}", [P, 512], F32)) for i in range(4)]
        psX = [ctx.enter_context(nc.psum_tensor(f"psX{i}", [P, 512], F32)) for i in range(4)]

        a_dram = nc.dram_tensor("a_dram", [EARLY, P, 4, S], F32).ap()
        mod_dram = nc.dram_tensor("mod_dram", [1, 6 * D], F32).ap()
        g_dram = nc.dram_tensor("g_dram", [NGRP, P, 32, P], F32).ap()

        consts_in = sem("consts_in")
        x_in = sem("x_in")
        stage_in = [sem("stage_in0"), sem("stage_in1")]
        mod_stored = sem("mod_stored")
        par_in = sem("par_in")
        x2_in = sem("x2_in")
        keys_in = sem("keys_in")
        g_stored = [sem("g_stored0"), sem("g_stored1")]
        g_in = sem("g_in")
        bs_in = sem("bs_in")
        b_cond_in = [sem("b_cond_in0"), sem("b_cond_in1")]
        cond_in = [sem(f"cond_in{r}") for r in range(4)]
        a_stored = [sem(f"a_stored{r}") for r in range(4)]
        a_in = sem("a_in")
        out_stored = sem("out_stored")
        zeroed = sem("zeroed")
        ident_ready = sem("ident_ready")
        tanh_c = sem("tanh_c")
        crep_ready = sem("crep_ready")
        mask_ready = sem("mask_ready")
        var_ready = sem("var_ready")
        std_ready = sem("std_ready")
        norm_ready = sem("norm_ready")
        th_ready = sem("th_ready")
        h_split = sem("h_split")
        y_norm = sem("y_norm")
        pool_step = sem("pool_step")
        hi_done = sem("hi_done")
        lo_done = sem("lo_done")
        tile_ready = sem("tile_ready")
        tile_free = sem("tile_free")
        aux_ready = sem("aux_ready")
        aux_free = sem("aux_free")
        act_ready = sem("act_ready")
        ev_free = sem("ev_free")
        x1_ready = sem("x1_ready")
        sc_ready = sem("sc_ready")
        sc_free = sem("sc_free")
        sc_used = sem("sc_used")
        s_shift = sem("s_shift")
        s_exp = sem("s_exp")
        gate_ready = sem("gate_ready")
        oh_keys_ready = sem("oh_keys_ready")
        oh_ready = sem("oh_ready")
        g_ready = sem("g_ready")
        g_free = sem("g_free")
        a_free = sem("a_free")
        g_used = sem("g_used")
        v_ready = sem("v_ready")
        v_free = sem("v_free")
        y_ready = sem("y_ready")
        dve_step = sem("dve_step")

        block = ctx.enter_context(nc.Block())

        def wait(eng, s, value):
            if not isinstance(value, int) or value > 0:
                eng.wait_ge(s, value)

        def front_units(rows):
            return w_front[rows].rearrange("p k n -> p (k n)")

        @block.sync
        def _(sp):
            sp.dma_start(ccol[:, :], c_col).then_inc(consts_in, 16)
            for u in range(2):
                sp.dma_start(stage[:, u, :], w_cond[u]).then_inc(stage_in[u], 16)
            sp.dma_start(xt, x.rearrange("(b p) d -> p b d", p=P)).then_inc(x_in, 16)
            sp.dma_start(mod[:, 0:2 * D], b_cond[0:2 * D].partition_broadcast(P)).then_inc(b_cond_in[0], 16)
            with sp.Fori(1, COND1 // 2) as i:
                for u in range(2):
                    sp.wait_ge(aux_ready, i * 2 + (u - 1))
                    sp.dma_start(stage[:, u, :], w_cond[i * 2 + u]).then_inc(stage_in[u], 16)
            for u in range(2):
                sp.wait_ge(aux_ready, COND1 - 1 + u)
                sp.dma_start(stage[:, u, :], front_units(u)).then_inc(stage_in[u], 16)
            for r in range(4):
                sp.dma_start(cond_ring[:, r, :], w_cond[COND1 + r]).then_inc(cond_in[r], 16)
            sp.dma_start(mod[:, 2 * D:6 * D], b_cond[2 * D:6 * D].partition_broadcast(P)).then_inc(b_cond_in[1], 16)
            sp.dma_start(cw[:, :, :], conv_w).then_inc(consts_in, 16)
            sp.dma_start(par[:, 0, :], ln_g.partition_broadcast(P)).then_inc(consts_in, 16)
            sp.dma_start(par[:, 1, :], ln_b.partition_broadcast(P)).then_inc(consts_in, 16)
            sp.dma_start(ws_t, w_spat).then_inc(consts_in, 16)
            sp.wait_ge(h_split, 16)
            sp.dma_start(bs_b.rearrange("p g i -> p (g i)"), b_spat.partition_broadcast(P)).then_inc(bs_in, 16)

            def load_front(n, u):
                sp.wait_ge(lo_done, n - 1)
                sp.dma_start(stage[:, u, :], front_units(n)).then_inc(stage_in[u], 16)

            def load_pairs(first, last):
                with sp.Fori(first // 2, last // 2) as i:
                    for u in range(2):
                        load_front(i * 2 + u, u)

            for v in range(N_V):
                load_front(v + 2, v % 2)
                if v + 1 < N_V:
                    for r in range(4):
                        sp.wait_ge(aux_ready, A_COND2 + 4 * v + r + 1)
                        sp.dma_start(cond_ring[:, r, :], w_cond[COND1 + 4 * (v + 1) + r]).then_inc(cond_in[r], 16)
            sp.wait_ge(aux_free, A_MIX)
            sp.dma_start(mod_dram, mod[0:1, :]).then_inc(mod_stored, 16)
            load_pairs(U_CONV + 2, U_O + 2)
            sp.wait_ge(tile_ready, T_O - 4)
            sp.wait_ge(mod_stored, 16)
            sp.dma_start(par[:, 0, :], mod_dram[0, 2 * D:3 * D].partition_broadcast(P)).then_inc(par_in, 16)
            sp.dma_start(x2, x.rearrange("(b p) d -> p b d", p=P)).then_inc(x2_in, 16)
            sp.dma_start(par[:, 1, :], ln1_g.partition_broadcast(P)).then_inc(par_in, 16)
            sp.dma_start(par[:, 2, :], ln1_b.partition_broadcast(P)).then_inc(par_in, 16)
            load_pairs(U_O + 2, U_O + 4)

            def load_u(n, e, p):
                sp.wait_ge(lo_done, n - 1)
                sp.dma_start(stage[:, p, :], u_units[e]).then_inc(stage_in[p], 16)

            def load_v(n, g, half):
                sp.wait_ge(lo_done, n - 1)
                sp.dma_start(stage[:, half, :].rearrange("p (j d) -> p j d", j=4),
                             expert_v[g][:, :, half * HT:half * HT + HT]).then_inc(stage_in[half], 16)

            def load_q(n, h):
                sp.wait_ge(lo_done, n - 1)
                sp.dma_start(stage[:, 0, :], front_units(h + U_Q)).then_inc(stage_in[0], 16)

            def load_gates(g):
                sp.dma_start(G_t, g_dram[g].rearrange("p n (j t) -> p n j t", j=4)).then_inc(g_in, 16)

            load_q(U_Q, 0)
            load_u(U_Q + 1, 0, 1)
            sp.wait_ge(x1_ready, 1)
            sp.dma_start(keys_sb, keys_t).then_inc(keys_in, 16)
            with sp.Fori(1, HEADS) as h:
                load_q(h * 2 + U_Q, h)
                load_u(h * 2 + (U_Q + 1), h, 1)
            for k in range(N_TAIL + 3):
                load_u(U_TAIL + k, HEADS + k, k % 2)

            def spread_unit(b4, n, load):
                for b in range(2):
                    sp.wait_ge(g_free, b4 * 8 + 8 * (b + 1))
                    sp.dma_start(g_dram[:, :, b4 + b, :].rearrange("g p n -> p g n"),
                                 gbuf[b].rearrange("p (g j) t -> p g (j t)", g=NGRP)).then_inc(g_stored[b], 16)
                load(n)

            with sp.Fori(0, 6) as i:
                for u in range(2):
                    spread_unit(i * 4 + 2 * u, i * 2 + (U_SPREAD + 3 + u),
                                lambda n: load_u(n, i * 2 + (HEADS + N_TAIL + 3 + u), (1 + u) % 2))
            for k in range(3):
                spread_unit(24 + 2 * k, U_POST - 1 + k, lambda n: load_u(n, 2 * EARLY - 3 + k, (1 + k) % 2))
            spread_unit(30, U_VE, lambda n: load_v(n, 0, 0))
            for b in range(2):
                sp.wait_ge(g_stored[b], 16 * 16)
            for r in range(4):
                sp.wait_ge(a_stored[r], 16 * 2)
            sp.dma_start(A_t, a_dram[0]).then_inc(a_in, 16)
            load_gates(0)
            load_v(U_VE + 1, 0, 1)
            load_v(U_VE + 2, 1, 0)
            for r in range(4):
                sp.wait_ge(a_stored[r], 16 * 2 * EARLY)

            def next_early(c):
                sp.wait_ge(a_free, c + 1)
                sp.dma_start(A_t, a_dram[c + 1]).then_inc(a_in, 16)
                sp.wait_ge(g_used, c + 1)
                load_gates(c + 1)
                load_v(c * 2 + (U_VE + 3), c + 1, 1)

            with sp.Fori(0, EARLY - 2) as c:
                next_early(c)
                load_v(c * 2 + (U_VE + 4), c + 2, 0)
            next_early(EARLY - 2)
            load_u(U_LATE, 2 * EARLY, 0)
            sp.wait_ge(g_used, EARLY)
            load_gates(EARLY)
            load_u(U_LATE + 1, 2 * EARLY + 1, 1)
            sp.wait_ge(sc_ready, 4 * HEADS)
            sp.dma_start(par[:, 0, :], mod_dram[0, 5 * D:6 * D].partition_broadcast(P)).then_inc(par_in, 16)
            sp.dma_start(par[:, 1, :], ln2_g.partition_broadcast(P)).then_inc(par_in, 16)
            sp.dma_start(par[:, 2, :], ln2_b.partition_broadcast(P)).then_inc(par_in, 16)
            with sp.Fori(0, NGRP - 1 - EARLY) as i:
                for half in range(2):
                    load_u(i * 4 + (U_LATE + 2 + half), i * 2 + (2 * EARLY + 2 + half), half)
                for half in range(2):
                    load_v(i * 4 + (U_LATE + 4 + half), i + EARLY, half)
                sp.wait_ge(g_used, i + (EARLY + 1))
                load_gates(i + (EARLY + 1))
            for half in range(2):
                load_v(U_LAST + half, NGRP - 1, half)
            for b in range(NB):
                sp.wait_ge(y_ready, b + 1)
                sp.dma_start(out[b * P:(b + 1) * P, :], xt[:, b, :]).then_inc(out_stored, 16)
            sp.wait_ge(out_stored, 16 * NB)

        @block.gpsimd
        def _(pool):
            pool.memset(ident[:, :], 0.0).then_inc(zeroed, 1)
            pool.wait_ge(zeroed, 1)
            pool.affine_select(out=ident[:, :], in_=ident[:, :], compare_op=ALU.not_equal, fill=1.0, base=0,
                               pattern=[[-1, P]], channel_multiplier=1).then_inc(ident_ready, 1)
            pool.iota(iota_i[:, :], pattern=[[1, P]], base=0, channel_multiplier=0).then_inc(ident_ready, 1)
            pool.wait_ge(consts_in, 16 * 5)
            pool.wait_ge(ident_ready, 2)
            pool.memset(ws_t[64:P, :, 0:64], 0.0).then_inc(mask_ready, 1)

            def store_acts(t, g, half):
                for r in range(4):
                    pool.wait_ge(tile_free, t + (r + 1))
                    pool.dma_start(a_dram[g, :, 2 * half + r // 2, (r % 2) * HT:(r % 2 + 1) * HT],
                                   ring[:, r, :]).then_inc(a_stored[r], 16)

            with pool.Fori(0, HEADS // 2) as i:
                for half in range(2):
                    store_acts(i * 16 + (T_Q + 8 * half + 4), i, half)
            with pool.Fori(0, EARLY - HEADS // 2) as i:
                for half in range(2):
                    store_acts(i * 8 + (T_TAIL + 4 * half), i + HEADS // 2, half)
            for b in range(NB):
                pool.wait_ge(y_norm, b + 1)
                pool.tensor_tensor(xt[:, b, :], xt[:, b, :], par[:, 1, :], ALU.mult).then_inc(pool_step, 1)
                pool.wait_ge(pool_step, b + 1)
                pool.tensor_tensor(xt[:, b, :], xt[:, b, :], par[:, 2, :], ALU.add).then_inc(y_ready, 1)

        @block.scalar
        def _(act):
            def make_hi(p, pair):
                act.wait_ge(stage_in[p], pair * 16 + 16 * (COND1 // 2 + 1))
                nc.scalar.activation(w_hi[:, p, :], stage[:, p, :], ACT.Copy, scale=WS).then_inc(hi_done, 1)

            def evacuate(t, dst, src, func=ACT.Copy, scale=DESCALE):
                act.wait_ge(tile_ready, t + 1)
                nc.scalar.activation(dst, src, func, scale=scale).then_inc(tile_free, 1)

            def root(k, blocks=slice(0, NB)):
                act.wait_ge(var_ready, k + 1)
                nc.scalar.activation(std[:, blocks], vare[:, blocks], ACT.Sqrt).then_inc(std_ready, 1)

            def feature_unit(t, dst, func=ACT.Copy, scale=DESCALE):
                for j in range(2):
                    for half in range(2):
                        evacuate(t + (2 * j + half), dst[:, j, half * HT:(half + 1) * HT],
                                 psU[2 * j + half][:, :], func, scale)

            def h_hi_tiles(first, done):
                for a in range(16):
                    k, half = a % 8, a // 8
                    act.wait_ge(aux_free, first + a + 1)
                    nc.scalar.activation(h_hi[:, k, half * HT:(half + 1) * HT], ring[:, a % 4, :],
                                         ACT.Copy).then_inc(th_ready, 1)

            act.wait_ge(consts_in, 16)
            nc.scalar.activation(cth[:, :], ccol[:, :], ACT.Tanh, scale=0.5).then_inc(tanh_c, 1)
            root(0)
            h_hi_tiles(A_HT, 0)
            for p in range(2):
                make_hi(p, 0)
            for u in range(N_V):
                for b in range(NB):
                    evacuate(T_V + 8 * u + b, xt[:, b, u * UC:(u + 1) * UC], psU[b % 4][:, 0:UC], ACT.Gelu_apprx_tanh)
                make_hi(u % 2, (u + 2) // 2)
            root(1)
            with act.Fori(0, 2) as i:
                for q in range(2):
                    for r, dst in enumerate((evAd, evB, evB)):
                        m = 3 * q + r
                        act.wait_ge(ev_free, i * 4 + (E_CONV + 2 * q + r // 2))
                        feature_unit(i * 24 + (T_CONV + 4 * m), dst)
                        make_hi(m % 2, i * 3 + (U_CONV + m + 2) // 2)
            for j in range(N_U):
                act.wait_ge(ev_free, E_U + max(0, j - 1))
                feature_unit(T_U + 4 * j, (evAd, evB)[j % 2], ACT.Gelu_apprx_tanh)
                make_hi(j % 2, (U_U + j + 2) // 2)
            with act.Fori(0, 4) as i:
                for r, dst in enumerate((evAd, evB, evC, evB)):
                    act.wait_ge(ev_free, i * 2 + (E_MERGE + r // 3))
                    if r % 2:
                        feature_unit(i * 16 + (T_MERGE + 4 * r), dst, ACT.Tanh, 0.5 * DESCALE)
                    else:
                        feature_unit(i * 16 + (T_MERGE + 4 * r), dst)
                    make_hi(r % 2, i * 2 + (U_MERGE + r + 2) // 2)
            for u in range(N_O):
                for b in range(NB):
                    evacuate(T_O + 8 * u + b, xt[:, b, u * UC:(u + 1) * UC], psU[b % 4][:, 0:UC])
                make_hi(u % 2, (U_O + u + 2) // 2)
            root(2)
            root(3, slice(0, 4))
            root(4, slice(4, 8))
            h_hi_tiles(A_H2T, 16)

            def early_acts(t, e):
                for r in range(4):
                    wait(act, a_stored[r], e * 16)
                    evacuate(t + r, ring[:, r, :], psU[r][:, :], ACT.Gelu_apprx_tanh)

            def heads(i):
                for q in range(2):
                    h = i * 2 + q
                    wait(act, sc_ready, i * 8 + 4 * (q - 1))
                    feature_unit(i * 16 + (T_Q + 8 * q), qb[q])
                    make_hi(0, h + (U_Q + 2) // 2)
                    wait(act, sc_used, h - 1)
                    for t in range(4):
                        act.wait_ge(sc_ready, i * 8 + (4 * q + t + 1))
                        nc.scalar.activation(sc[q][:, 2 * t:2 * t + 2, :, :].rearrange("p b h k -> p (b h k)"),
                                             psX[t][:, :], ACT.Copy).then_inc(sc_free, 1)
                    early_acts(i * 16 + (T_Q + 8 * q + 4), h)
                    make_hi(1, h + (U_Q + 2) // 2)

            heads(0)
            with act.Fori(1, HEADS // 2) as i:
                heads(i)
            for k in range(2):
                early_acts(T_TAIL + 4 * k, HEADS + k)
                make_hi(k, (U_TAIL + 2) // 2)
            act.wait_ge(s_shift, 1)
            s_flat = s_all.rearrange("p b h k -> p (b h k)")
            nc.scalar.activation(s_flat, s_flat, ACT.Exp).then_inc(s_exp, 1)
            for k in range(2, N_TAIL):
                early_acts(T_TAIL + 4 * k, HEADS + k)
                make_hi(k % 2, (U_TAIL + k + 2) // 2)

            def collect(i):
                for u in range(2):
                    e = i * 2 + (HEADS + N_TAIL + u)
                    for r in range(4):
                        wait(act, a_stored[r], e * 16)
                        evacuate(i * 8 + (T_SPREAD + 4 * u + r), ring[:, r, :], psU[r][:, :], ACT.Gelu_apprx_tanh)
                        b = r // 2
                        if r % 2 == 0:
                            wait(act, g_stored[b], i * 32 + 16 * u)
                        for q in range(4):
                            act.wait_ge(g_ready, i * 32 + (16 * u + 4 * r + q + 1))
                            at = 16 * (r % 2) + 4 * q
                            nc.scalar.activation(gbuf[b][:, :, at:at + 4],
                                                 psX[q][:, :].rearrange("p (t k) -> p k t", t=4),
                                                 ACT.Copy, scale=1.0 / GS).then_inc(g_free, 1)
                    make_hi(u, i + (U_SPREAD + 2) // 2)

            collect(0)
            with act.Fori(1, N_SPREAD // 2) as i:
                collect(i)

            for k in range(N_POST):
                early_acts(T_POST + 4 * k, HEADS + N_TAIL + N_SPREAD + k)
                make_hi(k, (U_POST + 2) // 2)

            def after_v(c, pair):
                for half in range(2):
                    act.wait_ge(v_ready, c * 16 + 8 * (half + 1))
                    make_hi(half, pair)

            with act.Fori(0, EARLY) as c:
                after_v(c, c + (U_VE + 2) // 2)

            def late_acts(t, g, pair):
                act.wait_ge(a_free, g)
                for half in range(2):
                    feature_unit(t + 4 * half, A_t[:, 2 * half:2 * half + 2, :], ACT.Gelu_apprx_tanh)
                    make_hi(half, pair)

            late_acts(T_LATE, EARLY, (U_LATE + 2) // 2)
            with act.Fori(0, NGRP - 1 - EARLY) as i:
                late_acts(i * 8 + (T_LATE + 8), i + (EARLY + 1), i * 2 + (U_LATE + 4) // 2)
                after_v(i + EARLY, i * 2 + (U_LATE + 6) // 2)
            for b in range(NB):
                root(5 + b, slice(b, b + 1))

        @block.vector
        def _(dve):
            V = nc.vector
            count = [0]
            base = [0]

            def step(ins):
                count[0] += 1
                return ins.then_inc(dve_step, 1)

            def settle():
                dve.wait_ge(dve_step, base[0] + count[0])

            def repeat(first, last, steps, body):
                start = count[0]
                with dve.Fori(first, last) as i:
                    base[0] = i * steps + (start - first * steps)
                    count[0] = 0
                    body(i)
                    assert count[0] == steps, (body, count[0])
                base[0] = 0
                count[0] = start + steps * (last - first)

            def make_lo(n, p):
                dve.wait_ge(hi_done, n + 1)
                V.scalar_tensor_tensor(w_lo[:, p, :], stage[:, p, :], WS, w_hi[:, p, :],
                                       ALU.mult, ALU.subtract).then_inc(lo_done, 1)

            def split(hi, lo, src, scale, done):
                step(V.tensor_scalar(hi, src, scale, None, ALU.mult))
                settle()
                V.scalar_tensor_tensor(lo, src, scale, hi, ALU.mult, ALU.subtract).then_inc(done, 1)

            def statistics(src, blocks=range(NB)):
                for b in blocks:
                    for half in range(2):
                        step(V.bn_stats(stats[:, b, half, :], src[:, b, half * HT:(half + 1) * HT]))
                settle()
                aggregate(blocks, 2)

            def aggregate(blocks, parts):
                for b in blocks:
                    step(V.bn_aggr(mv[:, b, :], stats[:, b, 0:parts, :]))
                settle()
                at = slice(blocks[0], blocks[-1] + 1)
                V.tensor_scalar(vare[:, at], mv[:, at, 1], EPS, None, ALU.add).then_inc(var_ready, 1)

            def normalise(k, dst, src, done, blocks=range(NB)):
                dve.wait_ge(std_ready, k + 1)
                at = slice(blocks[0], blocks[-1] + 1)
                step(V.reciprocal(rstd[:, at], std[:, at]))
                settle()
                for b in blocks:
                    ins = V.tensor_scalar(dst[:, b, :], src[:, b, :], mv[:, b, 0:1], rstd[:, b:b + 1],
                                          ALU.subtract, ALU.mult)
                    if done is None or b != blocks[-1]:
                        step(ins)
                    else:
                        ins.then_inc(done, 1)

            def row(ap, blocks=NB):
                return ap.unsqueeze(1).to_broadcast([P, blocks, ap.shape[1]])

            def split_h(first, before, shift, scale):
                for a in range(16 + 2):
                    if a < 16:
                        k = a % 8
                        dve.wait_ge(aux_ready, first + a + 1)
                        wait(dve, h_split, before + a - 3 if a >= 4 else 0)
                        V.tensor_scalar(ring[:, a % 4, :], psX[a % 4][:, :], cols[:, scale, k:k + 1],
                                        cols[:, shift, k:k + 1], ALU.mult, ALU.add).then_inc(aux_free, 1)
                    if a >= 2:
                        k, half = (a - 2) % 8, (a - 2) // 8
                        dve.wait_ge(th_ready, before + a - 1)
                        at = slice(half * HT, (half + 1) * HT)
                        V.tensor_tensor(h_lo[:, k, at], ring[:, (a - 2) % 4, :], h_hi[:, k, at],
                                        ALU.subtract).then_inc(h_split, 1)

            def columns(kind, start):
                settle()
                step(V.tensor_tensor(diag, mod[:, start * D:(start + 2) * D].rearrange("p (a b) -> p a b", b=P),
                                     ident[:, :].unsqueeze(1).to_broadcast([P, 2 * KD, P]), ALU.mult))
                settle()
                step(V.tensor_reduce(cols[:, kind:kind + 2, :].rearrange("p a k -> p (a k)"), diag, AX_X, ALU.add))
                settle()
                step(V.tensor_scalar(cols[:, kind, :], cols[:, kind, :], AS, None, ALU.mult))
                step(V.tensor_scalar(cols[:, kind + 1, :], cols[:, kind + 1, :], 1.0, AS, ALU.add, ALU.mult))
                settle()

            def cond_rows(u, a):
                dve.wait_ge(aux_ready, a + 1)
                part = mod[:, u * UC:(u + 1) * UC]
                V.tensor_tensor(part, psX[a % 4][:, 0:UC], part, ALU.add).then_inc(aux_free, 1)

            dve.wait_ge(ident_ready, 2)
            step(V.tensor_copy(iota_f[:, :], iota_i[:, 0:TOPK]))
            V.memset(evA[:, :, 0:2], 0.0).then_inc(ev_free, 1)
            dve.wait_ge(tanh_c, 1)
            step(V.tensor_scalar(cth[:, :], cth[:, :], 1.0, 0.5, ALU.add, ALU.mult))
            settle()
            step(V.tensor_tensor(cth[:, :], cth[:, :], ccol[:, :], ALU.mult))
            settle()
            V.tensor_copy(crep, cth[:, :].unsqueeze(2).to_broadcast([P, KD, P])).then_inc(crep_ready, 1)
            dve.wait_ge(x_in, 16)
            statistics(xt)
            normalise(0, xt, xt, norm_ready)
            dve.wait_ge(b_cond_in[0], 16)
            for u in range(COND1):
                cond_rows(u, u)
            dve.wait_ge(aux_free, COND1)
            columns(0, 0)
            split_h(A_HT, 0, 0, 1)
            make_lo(0, 0)
            make_lo(1, 1)
            dve.wait_ge(b_cond_in[1], 16)
            for v in range(N_V):
                dve.wait_ge(tile_free, T_V + 8 * (v + 1))
                make_lo(v + 2, v % 2)
                for r in range(4):
                    cond_rows(COND1 + 4 * v + r, A_COND2 + 4 * v + r)
            dve.wait_ge(aux_free, A_MIX)
            statistics(xt)
            normalise(1, xt, xt, None)
            settle()
            step(V.tensor_tensor(xt, xt, row(par[:, 0, :]), ALU.mult))
            settle()
            V.tensor_tensor(xt, xt, row(par[:, 1, :]), ALU.add).then_inc(norm_ready, 1)
            columns(2, 3)

            def conv(i):
                for q in range(2):
                    qc = i * 4 + 2 * q
                    m = 3 * q
                    t = i * 24 + (T_CONV + 4 * m)
                    n = i * 6 + (U_CONV + m + 2)
                    make_lo(n, m % 2)
                    make_lo(n + 1, (m + 1) % 2)
                    dve.wait_ge(tile_free, t + 8)
                    V.tensor_tensor(evAd, evAd, evB, ALU.mult).then_inc(ev_free, 1)
                    dve.wait_ge(ev_free, i * 4 + (E_CONV + 2 * q + 1))

                    def weight(j, tap):
                        return cw[:, bass.ds(qc + j, 1), tap:tap + 1].rearrange("p a b -> p (a b)")

                    for j in range(2):
                        step(V.tensor_scalar(evC[:, j, :], evA[:, j, 0:S], weight(j, 0), None, ALU.mult))
                    settle()
                    for tap in (1, 2):
                        for j in range(2):
                            step(V.scalar_tensor_tensor(evC[:, j, :], evA[:, j, tap:tap + S], weight(j, tap),
                                                        evC[:, j, :], ALU.mult, ALU.add))
                        settle()
                    make_lo(n + 2, m % 2)
                    dve.wait_ge(tile_free, t + 12)
                    step(V.tensor_tensor(evC, evC, evB, ALU.mult))
                    settle()
                    split(yb_hi[:, bass.ds(qc, 2), :], yb_lo[:, bass.ds(qc, 2), :], evC, AS, ev_free)

            repeat(0, 2, 16, conv)
            dve.wait_ge(bs_in, 16)
            dve.wait_ge(mod_stored, 16)
            for a in range(16):
                g, half = a // 2, a % 2
                dve.wait_ge(aux_ready, A_MIX + a + 1)
                V.tensor_tensor(mixb[:, g, half * HT:(half + 1) * HT].rearrange("p (n i) -> p n i", n=4),
                                psX[a % 4][:, :].rearrange("p (n i) -> p n i", n=4),
                                bs_b[:, g:g + 1, :].to_broadcast([P, 4, P]), ALU.add).then_inc(aux_free, 1)
            dve.wait_ge(aux_free, A_H2T)
            for j in range(N_U):
                make_lo(U_U + j + 2, j % 2)
                dve.wait_ge(tile_free, T_U + 4 * (j + 1))
                ev = (evAd, evB)[j % 2]
                step(V.tensor_tensor(ev, ev, mixb[:, 2 * j:2 * j + 2, :], ALU.mult))
                settle()
                split(ya_hi[:, 2 * j:2 * j + 2, :], ya_lo[:, 2 * j:2 * j + 2, :], ev, AS, ev_free)

            def merge(i):
                qc = i * 2
                t = i * 16 + T_MERGE
                n = i * 4 + (U_MERGE + 2)
                make_lo(n, 0)
                make_lo(n + 1, 1)
                dve.wait_ge(tile_free, t + 8)
                V.scalar_tensor_tensor(evAd, evB, 1.0, evAd, ALU.add, ALU.mult).then_inc(ev_free, 1)
                make_lo(n + 2, 0)
                make_lo(n + 3, 1)
                dve.wait_ge(tile_free, t + 16)
                step(V.scalar_tensor_tensor(evC, evB, 1.0, evC, ALU.add, ALU.mult))
                settle()
                dve.wait_ge(ev_free, i * 2 + (E_MERGE + 1))
                step(V.tensor_tensor(evAd, evAd, evC, ALU.add))
                settle()
                split(m_hi[:, bass.ds(qc, 2), :], m_lo[:, bass.ds(qc, 2), :], evAd, 0.5 * AS, ev_free)

            repeat(0, 4, 3, merge)
            dve.wait_ge(par_in, 16 * 3)
            dve.wait_ge(x2_in, 16)
            for u in range(N_O):
                make_lo(U_O + u + 2, u % 2)
                dve.wait_ge(tile_free, T_O + 8 * (u + 1))
                at = slice(u * UC, (u + 1) * UC)
                step(V.tensor_tensor(xt[:, :, at], xt[:, :, at], row(par[:, 0, at]), ALU.mult))
                settle()
                step(V.scalar_tensor_tensor(xt[:, :, at], x2[:, :, at], ALPHA, xt[:, :, at], ALU.mult, ALU.add))
                settle()
                for b in range(NB):
                    step(V.bn_stats(stats[:, b, u, :], xt[:, b, at]))
            settle()
            aggregate(range(NB), N_O)
            normalise(2, xt, xt, None)
            settle()
            halves = (range(0, 4), range(4, 8))
            for k, blocks in enumerate(halves):
                part = xt[:, 4 * k:4 * k + 4, :]
                step(V.tensor_tensor(part, part, row(par[:, 1, :], 4), ALU.mult))
                settle()
                if k == 0:
                    step(V.tensor_tensor(part, part, row(par[:, 2, :], 4), ALU.add))
                    settle()
                else:
                    V.tensor_tensor(part, part, row(par[:, 2, :], 4), ALU.add).then_inc(x1_ready, 1)
                    dve.wait_ge(x1_ready, 1)
                statistics(xt, blocks)
            for k, blocks in enumerate(halves):
                normalise(3 + k, x2, xt, norm_ready, blocks)
            split_h(A_H2T, 16, 2, 3)

            def alone():
                V.memset(unread[:, :], 0.0)

            def best16(items):
                alone()
                for v, p, src, s in items:
                    step(V.max(v[:, 0:8], src))
                settle()
                alone()
                for v, p, src, s in items:
                    step(V.max_index(p[:, 0:8], v[:, 0:8], src))
                    step(V.match_replace(s, v[:, 0:8], src, LOWEST))
                settle()
                alone()
                for v, p, src, s in items:
                    step(V.max(v[:, 8:16], s))
                settle()
                alone()
                for v, p, src, s in items:
                    step(V.max_index(p[:, 8:16], v[:, 8:16], s))
                settle()

            def rank(i):
                for q in range(2):
                    h = i * 2 + q
                    s = sc[q]
                    make_lo(i * 4 + (U_Q + 2 * q + 2), 0)
                    dve.wait_ge(sc_free, i * 8 + 4 * (q + 1))
                    best16([(vals[:, b, a, :], idx[:, b, a, :], s[:, b, a, :], sc2[:, b, a, :])
                            for b in range(NB) for a in range(2)])
                    V.tensor_copy(idxf, idx).then_inc(sc_used, 1)
                    make_lo(i * 4 + (U_Q + 2 * q + 3), 1)
                    step(V.tensor_tensor(cand, vals[:, :, 0, :].unsqueeze(3).to_broadcast([P, NB, TOPK, TOPK]),
                                         vals[:, :, 1, :].unsqueeze(2).to_broadcast([P, NB, TOPK, TOPK]), ALU.add))
                    settle()
                    best16([(tops[:, b, :], sel[:, b, :], cand[:, b, :, :].rearrange("p i j -> p (i j)"),
                             cand2[:, b, :]) for b in range(NB)])

                    def slot(dst):
                        return dst[:, :, bass.ds(h, 1), :].rearrange("p b h k -> p b (h k)")

                    step(V.tensor_copy(slot(s_all), tops))
                    sel_flat = sel.rearrange("p b k -> p (b k)")
                    step(V.tensor_scalar(sel_a, sel_flat, 4, None, ALU.logical_shift_right))
                    step(V.tensor_scalar(sel_b, sel_flat, 15, None, ALU.bitwise_and))
                    settle()
                    step(V.tensor_copy(sel_af, sel_a))
                    step(V.tensor_copy(sel_bf, sel_b))
                    settle()
                    dve.wait_ge(sc_used, h + 1)
                    for half, place, dst in ((0, sel_af, i1_all), (1, sel_bf, i2_all)):
                        step(V.tensor_tensor(cmp_t, place.unsqueeze(2).to_broadcast([P, NB * TOPK, TOPK]),
                                             iota_f[:, :].unsqueeze(1).to_broadcast([P, NB * TOPK, TOPK]), ALU.is_equal))
                        settle()
                        by_block = cmp_t.rearrange("p (b k) j -> p b k j", b=NB)
                        step(V.tensor_tensor(by_block, by_block,
                                             idxf[:, :, half, :].unsqueeze(2).to_broadcast([P, NB, TOPK, TOPK]), ALU.mult))
                        settle()
                        step(V.tensor_reduce(slot(dst), by_block, AX_X, ALU.add))
                        settle()

            repeat(0, HEADS // 2, 264, rank)
            s3 = s_all.rearrange("p b h k -> p (b h) k")
            rows3 = [P, NB * HEADS, TOPK]
            step(V.tensor_copy(rsum, s3[:, :, 0]))
            settle()
            V.tensor_tensor(s3, s3, rsum.unsqueeze(2).to_broadcast(rows3), ALU.subtract).then_inc(s_shift, 1)
            for k in range(2):
                make_lo(U_TAIL + 2 + k, k)
            dve.wait_ge(s_exp, 1)
            step(V.tensor_reduce(rsum, s3, AX_X, ALU.add))
            settle()
            step(V.reciprocal(rinv, rsum))
            settle()
            V.tensor_tensor(s3, s3, rinv.unsqueeze(2).to_broadcast(rows3), ALU.mult).then_inc(gate_ready, 1)
            make_lo(U_SPREAD, 0)
            step(V.tensor_copy(iota_k4, iota_i[:, :].unsqueeze(2).to_broadcast([P, P, 4])))
            for a in range(6):
                kind, half = a // 2, a % 2
                at = slice(half * HT, (half + 1) * HT)
                dve.wait_ge(aux_ready, A_IDX + a + 1)
                if kind < 2:
                    V.tensor_copy(keys_t16[:, kind, at], psX[a % 4][:, :]).then_inc(aux_free, 1)
                else:
                    V.tensor_scalar(g_t[:, at], psX[a % 4][:, :], GS, None, ALU.mult).then_inc(aux_free, 1)
            dve.wait_ge(aux_free, A_END)
            step(V.tensor_copy(gates16[:, 0, :], g_t))
            settle()
            step(V.tensor_tensor(gates16[:, 1, :], g_t, gates16[:, 0, :], ALU.subtract))
            settle()

            def onehots(i):
                def tokens(src, u, q):
                    at = src[:, :, bass.ds(i * 128 + (64 * u + 4 * q), 4)]
                    return at.unsqueeze(2).to_broadcast([P, 2, P, 4])

                def gate(u, q):
                    dve.wait_ge(oh_keys_ready, i * 32 + (16 * u + q + 1))
                    both = oh_keys[:, q % 4, 1:2, :, :].to_broadcast([P, 2, P, 4])
                    V.tensor_tensor(oh_gate[:, q % 4, :, :, :], both, tokens(gates16, u, q), ALU.mult).then_inc(oh_ready, 1)

                for u in range(2):
                    for q in range(16):
                        if q == 4:
                            make_lo(i * 2 + (U_SPREAD + u + 1), (u + 1) % 2)
                        wait(dve, g_ready, i * 32 + (16 * u + q - 3))
                        keys = iota_k4.unsqueeze(1).to_broadcast([P, 2, P, 4])
                        V.tensor_tensor(oh_keys[:, q % 4, :, :, :], keys, tokens(keys_t16, u, q),
                                        ALU.is_equal).then_inc(oh_keys_ready, 1)
                        if q:
                            gate(u, q - 1)
                    gate(u, 15)

            onehots(0)
            with dve.Fori(1, N_SPREAD // 2) as i:
                onehots(i)
            make_lo(U_POST + 1, 1)
            dve.wait_ge(g_ready, 256)
            step(V.memset(R3[:, 4096:4096 + 8192], 0.0))
            settle()
            make_lo(U_VE, 0)

            def coefficients(g, p):
                def product(j):
                    if j == 0:
                        dve.wait_ge(g_in, g * 16 + 16)
                    a = A_t[:, j, :].rearrange("p (n t) -> p n t", n=32)
                    ins = V.scalar_tensor_tensor(a, a, AS, G_t[:, :, j, :], ALU.mult, ALU.mult)
                    if j < 3:
                        step(ins)
                    else:
                        ins.then_inc(g_used, 1)

                def hi():
                    dve.wait_ge(g_used, g + 1)
                    settle()
                    step(V.tensor_scalar(c_hi[p], A_t, 1.0, None, ALU.mult))

                def lo():
                    settle()
                    V.tensor_tensor(c_lo[p], A_t, c_hi[p], ALU.subtract).then_inc(a_free, 1)

                return [lambda j=j: product(j) for j in range(4)] + [hi, lo]

            def gather_out(c, n, between=()):
                between = list(between)
                for half in range(2):
                    for b in range(NB):
                        dve.wait_ge(v_ready, c * 16 + (8 * half + b + 1))
                        dst = acc[:, b, half * HT:(half + 1) * HT]
                        V.tensor_tensor(dst, psX[b % 4][:, :], dst, ALU.add).then_inc(v_free, 1)
                        if between:
                            between.pop(0)()
                    make_lo(n + half, half)

            def early(g, p):
                def start():
                    dve.wait_ge(a_in, g * 16 + 32)
                pieces = coefficients(g + 1, 1 - p)
                first = pieces[0]
                pieces[0] = lambda: (start(), first())
                gather_out(g, g * 2 + (U_VE + 2), pieces)

            def late(g, p, n, t):
                dve.wait_ge(tile_free, t)
                for piece in coefficients(g, p):
                    piece()
                make_lo(n, 0)
                make_lo(n + 1, 1)
                gather_out(g, n + 2)

            dve.wait_ge(a_in, 16)
            for piece in coefficients(0, 0):
                piece()
            make_lo(U_VE + 1, 1)

            def early_pair(i):
                for p in range(2):
                    early(i * 2 + p, p)

            repeat(0, (EARLY - 1) // 2, 8, early_pair)
            gather_out(EARLY - 1, U_LATE)
            for p in range(2):
                make_lo(U_LATE + 2 + p, p)

            def late_pair(i):
                for k in range(2):
                    late(i * 2 + (EARLY + k), (EARLY + k) % 2, i * 8 + (U_LATE + 4 + 4 * k),
                         i * 16 + (T_LATE + 8 * (k + 1)))

            repeat(0, (NGRP - 1 - EARLY) // 2, 8, late_pair)
            dve.wait_ge(tile_free, T_LATE + 8 * (NGRP - EARLY))
            for piece in coefficients(NGRP - 1, (NGRP - 1) % 2):
                piece()
            dve.wait_ge(par_in, 16 * 6)

            def finish(b):
                normalise(5 + b, xt, xt, y_norm, range(b, b + 1))

            for half in range(2):
                for b in range(NB):
                    dve.wait_ge(v_ready, 16 * (NGRP - 1) + 8 * half + b + 1)
                    dst = acc[:, b, half * HT:(half + 1) * HT]
                    V.tensor_tensor(dst, psX[b % 4][:, :], dst, ALU.add).then_inc(v_free, 1)
                    if half:
                        dve.wait_ge(v_free, 16 * (NGRP - 1) + 8 * half + b + 1)
                        step(V.scalar_tensor_tensor(acc[:, b, :], acc[:, b, :], DESCALE, par[:, 0, :], ALU.mult, ALU.mult))
                        settle()
                        step(V.scalar_tensor_tensor(xt[:, b, :], xt[:, b, :], ALPHA, acc[:, b, :], ALU.mult, ALU.add))
                        settle()
                        statistics(xt, range(b, b + 1))
                        if b:
                            finish(b - 1)
            finish(NB - 1)

        @block.tensor
        def _(pe):
            mm = nc.tensor.matmul

            def aux_tile(a):
                wait(pe, aux_free, a - 3)
                return psX[a % 4]

            def product(ps, lhs, rhs, chunks):
                n = len(chunks)
                for s, k in enumerate(chunks):
                    mm(ps, lhs[0](k), rhs[0](k), start=(s == 0), stop=False)
                    mm(ps, lhs[0](k), rhs[1](k), start=False, stop=False)
                    last = mm(ps, lhs[1](k), rhs[0](k), start=False, stop=(s == n - 1))
                return last

            def w_unit(p, columns):
                return [w[:, p, :].rearrange("p (k n) -> p k n", n=columns) for w in (w_hi, w_lo)]

            def feature_unit(n, p, t, hi, lo, between=None):
                pe.wait_ge(lo_done, n + 1)
                w = w_unit(p, UC)
                for j in range(2):
                    for half in range(2):
                        r = 2 * j + half
                        wait(pe, tile_free, t + (r - 3))
                        product(psU[r][:, :],
                                [lambda k, s=s: w[s][:, k, j * P:(j + 1) * P] for s in range(2)],
                                [lambda k, s=s: (hi, lo)[s][:, k, half * HT:(half + 1) * HT] for s in range(2)],
                                range(KD)).then_inc(tile_ready, 1)
                        if between:
                            between(r)

            def token_unit(n, p, t, hi, lo):
                pe.wait_ge(lo_done, n + 1)
                w = w_unit(p, UC)
                for b in range(NB):
                    wait(pe, tile_free, t + (b - 3))
                    product(psU[b % 4][:, 0:UC],
                            [lambda k, s=s: (hi, lo)[s][:, k, b * P:(b + 1) * P] for s in range(2)],
                            [lambda k, s=s: w[s][:, k, :] for s in range(2)],
                            range(KD)).then_inc(tile_ready, 1)

            def transposes(first, src, half):
                for k in range(KD):
                    ps = aux_tile(first + 8 * half + k)
                    for b in range(4):
                        ins = nc.tensor.transpose(ps[:, b * P:(b + 1) * P], src[:, 4 * half + b, k * P:(k + 1) * P],
                                                  ident[:, :])
                    ins.then_inc(aux_ready, 1)

            def cond_unit(w, a):
                w = w.rearrange("p (k n) -> p k n", k=KD)
                ps = aux_tile(a)
                for k in range(KD):
                    ins = mm(ps[:, 0:UC], crep[:, k, :], w[:, k, :], start=(k == 0), stop=(k == KD - 1))
                ins.then_inc(aux_ready, 1)

            pe.wait_ge(crep_ready, 1)
            for u in range(COND1):
                pe.wait_ge(stage_in[u % 2], 16 * (u // 2 + 1))
                cond_unit(stage[:, u % 2, :], u)
            pe.wait_ge(ident_ready, 2)
            pe.wait_ge(norm_ready, 1)
            for half in range(2):
                transposes(A_HT, xt, half)
            pe.wait_ge(h_split, 16)
            for u in range(N_V):
                token_unit(U_V + u, u % 2, T_V + 8 * u, h_hi, h_lo)
                for r in range(4):
                    pe.wait_ge(cond_in[r], 16 * (u + 1))
                    cond_unit(cond_ring[:, r, :], A_COND2 + 4 * u + r)
            with pe.Fori(0, N_CONV // 2) as i:
                for p in range(2):
                    feature_unit(i * 2 + (U_CONV + p), p, i * 8 + (T_CONV + 4 * p), h_hi, h_lo)
            pe.wait_ge(norm_ready, 2)
            pe.wait_ge(mask_ready, 1)
            for a in range(16):
                g, half = a // 2, a % 2
                ps = aux_tile(A_MIX + a)
                for b in range(4):
                    ins = mm(ps[:, b * P:(b + 1) * P], xt[:, 4 * half + b, g * P:(g + 1) * P], ws_t[:, g, :],
                             start=True, stop=True)
                ins.then_inc(aux_ready, 1)
            with pe.Fori(0, N_U // 2) as i:
                for p in range(2):
                    feature_unit(i * 2 + (U_U + p), p, i * 8 + (T_U + 4 * p), h_hi, h_lo)
            pe.wait_ge(ev_free, E_MERGE)
            with pe.Fori(0, 4) as i:
                for r, (hi, lo) in enumerate(((ya_hi, ya_lo), (h_hi, h_lo), (yb_hi, yb_lo), (h_hi, h_lo))):
                    feature_unit(i * 4 + (U_MERGE + r), r % 2, i * 16 + (T_MERGE + 4 * r), hi, lo)
            pe.wait_ge(ev_free, E_END)
            for u in range(N_O):
                token_unit(U_O + u, u % 2, T_O + 8 * u, m_hi, m_lo)
            for half in range(2):
                pe.wait_ge(norm_ready, 3 + half)
                transposes(A_H2T, x2, half)
            pe.wait_ge(h_split, 32)
            pe.wait_ge(keys_in, 16)

            def heads(i):
                for q in range(2):
                    feature_unit(i * 4 + (U_Q + 2 * q), 0, i * 16 + (T_Q + 8 * q), h_hi, h_lo)
                    pe.wait_ge(tile_free, i * 16 + (T_Q + 8 * q + 4))
                    for t in range(4):
                        wait(pe, sc_free, i * 8 + (4 * (q - 1) + t + 1))
                        for m in range(4):
                            b, half = 2 * t + m // 2, m % 2
                            keys = keys_sb[:, bass.ds(i * 4 + (2 * q + half), 1), :].rearrange("p a k -> p (a k)")
                            ins = mm(psX[t][:, m * P:(m + 1) * P], qb[q][:, half, b * P:(b + 1) * P], keys,
                                     start=True, stop=True)
                        ins.then_inc(sc_ready, 1)
                    feature_unit(i * 4 + (U_Q + 2 * q + 1), 1, i * 16 + (T_Q + 8 * q + 4), h_hi, h_lo)

            heads(0)
            with pe.Fori(1, HEADS // 2) as i:
                heads(i)
            for k in range(N_TAIL - 1):
                feature_unit(U_TAIL + k, k % 2, T_TAIL + 4 * k, h_hi, h_lo)
            pe.wait_ge(gate_ready, 1)
            pe.wait_ge(sc_free, 4 * HEADS)
            for a in range(6):
                kind, half = a // 2, a % 2
                ps = aux_tile(A_IDX + a)
                src = (i1_all, i2_all, s_all)[kind].rearrange("p b h k -> p b (h k)")
                for b in range(4):
                    ins = nc.tensor.transpose(ps[:, b * P:(b + 1) * P], src[:, 4 * half + b, :], ident[:, :])
                ins.then_inc(aux_ready, 1)
            feature_unit(U_SPREAD - 1, 1, T_SPREAD - 4, h_hi, h_lo)
            pe.wait_ge(aux_free, A_END)

            def spread(i):
                for u in range(2):
                    def gates(r):
                        for q in range(4):
                            at = 16 * u + 4 * r + q
                            wait(pe, g_free, i * 32 + (at - 3))
                            pe.wait_ge(oh_ready, i * 32 + (at + 1))
                            for t in range(4):
                                for c in range(2):
                                    ins = mm(psX[q][:, t * P:(t + 1) * P], oh_keys[:, q, 0, :, t],
                                             oh_gate[:, q, c, :, t], start=(c == 0), stop=(c == 1))
                            ins.then_inc(g_ready, 1)
                    feature_unit(i * 2 + (U_SPREAD + u), u, i * 8 + (T_SPREAD + 4 * u), h_hi, h_lo, gates)

            spread(0)
            with pe.Fori(1, N_SPREAD // 2) as i:
                spread(i)
            for k in range(N_POST):
                feature_unit(U_POST + k, k, T_POST + 4 * k, h_hi, h_lo)
            pe.wait_ge(g_free, 256)

            def expert_out(n, c, p, first=False):
                pe.wait_ge(a_free, c + 1)
                for half in range(2):
                    pe.wait_ge(lo_done, n + (half + 1))
                    w = w_unit(half, HT)
                    for b in range(NB):
                        if not (first and half == 0 and b < 4):
                            pe.wait_ge(v_free, c * 16 + (8 * half + b - 3))
                        product(psX[b % 4][:, :],
                                [lambda k, s=s: (c_hi, c_lo)[s][p][:, k, b * P:(b + 1) * P] for s in range(2)],
                                [lambda k, s=s: w[s][:, k, :] for s in range(2)],
                                range(4)).then_inc(v_ready, 1)

            def expert_in(n, t):
                for half in range(2):
                    feature_unit(n + half, half, t + 4 * half, h_hi, h_lo)

            expert_out(U_VE, 0, 0, True)
            with pe.Fori(0, (EARLY - 1) // 2) as i:
                for p in range(2):
                    expert_out(i * 4 + (U_VE + 2 * (p + 1)), i * 2 + (p + 1), 1 - p)
            expert_in(U_LATE, T_LATE)
            with pe.Fori(0, (NGRP - 1 - EARLY) // 2) as i:
                for k in range(2):
                    expert_in(i * 8 + (U_LATE + 2 + 4 * k), i * 16 + (T_LATE + 8 * (k + 1)))
                    expert_out(i * 8 + (U_LATE + 4 + 4 * k), i * 2 + (EARLY + k), (EARLY + k) % 2)
            expert_out(U_LAST, NGRP - 1, (NGRP - 1) % 2)


def _unit_columns(w):
    return w.reshape(KD, P, -1, UC).transpose(2, 1, 0, 3)


def kernel(**inputs):
    import concourse.bacc as _bacc
    from concourse.bass_utils import run_bass_kernel_spmd as _run

    a = {k: np.asarray(v) for k, v in inputs.items()}
    w_in = _unit_columns(a["w_in"][0])
    part = {name: w_in[4 * i:4 * i + 4] for i, name in enumerate(("u", "v", "gB", "gC", "z", "ga", "gb"))}
    pa, pb = _unit_columns(a["p_a"][0]), _unit_columns(a["p_b"][0])
    order = list(part["v"])
    for q in range(4):
        order += [part["z"][q], part["gC"][q], part["gB"][q]]
    order += list(part["u"])
    for q in range(4):
        order += [pa[q], part["ga"][q], pb[q], part["gb"][q]]
    order += list(_unit_columns(a["w_o"][0])) + list(_unit_columns(a["w_q_peer"][0]))
    arrays = {
        "x": a["x"][0],
        "c_col": a["c"].reshape(KD, P).T,
        "w_cond": _unit_columns(a["w_cond"][0]).reshape(NCOND, P, 2048),
        "b_cond": a["b_cond"][0],
        "w_front": np.stack(order),
        "ln_g": a["gmlp_ln_g"][0],
        "ln_b": a["gmlp_ln_b"][0],
        "w_spat": a["w_spatial"][0].transpose(2, 0, 1),
        "b_spat": a["b_spatial"][0].reshape(-1),
        "conv_w": a["conv_w"][0].reshape(3, KD, P).transpose(2, 1, 0),
        "ln1_g": a["ln1_g"][0],
        "ln1_b": a["ln1_b"][0],
        "keys_t": a["sub_keys"][0].reshape(2 * HEADS, NKEYS, P).transpose(2, 0, 1),
        "u_units": a["expert_u"][0].reshape(P, NGRP, 2, 2, KD, P).transpose(1, 2, 5, 4, 3, 0).reshape(2 * NGRP, P, 2048),
        "expert_v": a["expert_v"][0],
        "ln2_g": a["ln2_g"][0],
        "ln2_b": a["ln2_b"][0],
    }
    nc = _bacc.Bacc("TRN2", target_bir_lowering=False, num_devices=1)
    arrays = {"in_" + k: np.ascontiguousarray(v) for k, v in arrays.items()}
    args = [nc.dram_tensor(k, v.shape, mybir.dt.from_np(v.dtype), kind="ExternalInput").ap() for k, v in arrays.items()]
    names = [k[3:] for k in arrays]
    args[names.index("expert_v")] = args[names.index("expert_v")].rearrange("(p g j) d -> g p j d", p=P, j=4)
    out = nc.dram_tensor("out", (S, D), F32, kind="ExternalOutput").ap()
    trunk_layer(nc, *args, out)
    r = _run(nc, [arrays], core_ids=[0])
    return r.results[0]["out"].reshape(1, S, D)
```

```python
from contextlib import ExitStack

import numpy as np

import concourse.bass as bass
from concourse import mybir

ALU = mybir.AluOpType
ACT = mybir.ActivationFunctionType
F32 = mybir.dt.float32
F16 = mybir.dt.float16
U32 = mybir.dt.uint32
I32 = mybir.dt.int32
AX_X = mybir.AxisListType.X

P = 128
D = 1024
S = 1024
KD = D // P
NB = S // P
GROUPS = 8
HEADS = 8
NKEYS = 128
TOPK = 16
HT = 512
UC = 256
ALPHA = 2.0 ** 0.25
EPS = 1e-5
WS = 256.0
AS = 16.0
DESCALE = 1.0 / (WS * AS)
GS = 4096.0
LOWEST = -3.0e38

NCOND = 6 * D // UC
N_V, N_CONV, N_U, N_MERGE, N_O = 4, 12, 4, 16, 4
U_V = 0
U_CONV = U_V + N_V
U_U = U_CONV + N_CONV
U_MERGE = U_U + N_U
U_O = U_MERGE + N_MERGE
U_Q = U_O + N_O
NGRP = 32
NSP = 2
DB = NB - NSP
DT = DB * P
HD = DT // 2
N_TAIL, N_SPREAD, N_POST = 6, DT // 64, 4
U_TAIL = U_Q + 3 * HEADS
U_SPREAD = U_TAIL + N_TAIL
U_POST = U_SPREAD + N_SPREAD
N_HEAD = 2 * HEADS
EARLY = (N_HEAD + N_TAIL + N_SPREAD + N_POST) // 2
U_VE = U_POST + N_POST
U_LATE = U_VE + 2 * EARLY
T_V = 0
T_CONV = T_V + 8 * N_V
T_U = T_CONV + 4 * N_CONV
T_MERGE = T_U + 4 * N_U
T_O = T_MERGE + 4 * N_MERGE
T_Q = T_O + 8 * N_O
T_TAIL = T_Q + 12 * HEADS
T_SPREAD = T_TAIL + 4 * N_TAIL
T_POST = T_SPREAD + 4 * N_SPREAD
T_LATE = T_POST + 4 * N_POST
U_LAST = U_LATE + 2 + 4 * (NGRP - 1 - EARLY)
COND1 = 2 * D // UC
A_HT = COND1
A_COND2 = A_HT + 16
A_MIX = NCOND + 16
A_H2T = A_MIX + 16
A_IDX = A_H2T + 16
A_END = A_IDX + 6
VT = 2 * DB
SLOTS = NSP * HEADS * TOPK
LAG = 16
K_EARLY, K_LATE = 4, 13
K_GAP = SLOTS - LAG - (EARLY - 1) * K_EARLY - (NGRP - 1 - EARLY) * K_LATE
S_GAP = (EARLY - 1) * K_EARLY
S_LATE = S_GAP + K_GAP
LATE_AHEAD = 14
END_ORDER = [*range(DB, NB), *range(DB)]
E_CONV = 1
E_U = E_CONV + 8
E_MERGE = E_U + 4
E_END = E_MERGE + 8


def trunk_layer(nc, x, c_col, w_cond, b_cond, w_front, ln_g, ln_b, w_spat, b_spat, conv_w,
                ln1_g, ln1_b, keys_t, u_units, u_rows, expert_v, v_rows, ln2_g, ln2_b, out):
    with ExitStack() as ctx:
        def sb(name, shape, dt=F32):
            return ctx.enter_context(nc.sbuf_tensor(name, shape, dt))

        def sem(name):
            return ctx.enter_context(nc.semaphore(name))

        stage = sb("stage", [P, 2, 2048])
        w_hi = sb("w_hi", [P, 2, 2048], F16)
        w_lo = sb("w_lo", [P, 2, 2048], F16)
        h_hi = sb("h_hi", [P, KD, S], F16)
        h_lo = sb("h_lo", [P, KD, S], F16)
        R1 = sb("R1", [P, 8192])
        R2 = sb("R2", [P, 8192])
        R3 = sb("R3", [P, 8192 + 2052 + 2048 + 2048])
        par = sb("par", [P, 3, D])
        ring = sb("ring", [P, 4, HT])
        ident = sb("ident", [P, P])
        iota_i = sb("iota_i", [P, P], I32)
        iota_f = sb("iota_f", [P, TOPK])
        cw = sb("cw", [P, KD, 3])
        ccol = sb("ccol", [P, KD])
        cth = sb("cth", [P, KD])
        cols = sb("cols", [P, 4, KD])
        stats = sb("stats", [P, NB, 4, 6])
        mv = sb("mv", [P, NB, 2])
        vare = sb("vare", [P, NB])
        std = sb("std", [P, NB])
        rstd = sb("rstd", [P, NB])
        unread = sb("unread", [P, 1])
        dots = sb("dots", [P, LAG])
        weight_sp = sb("weight_sp", [P, SLOTS])
        idx_now = sb("idx_now", [P, 2, max(K_LATE, K_GAP) + LAG], U32)
        carrier = sb("carrier", [P, 2])

        def view(region, at, n, dt=F32):
            v = region[:, at:at + n]
            return v.bitcast(dt) if dt != F32 else v

        def v3(ap, a):
            return ap.rearrange("p (a b) -> p a b", a=a)

        xt = v3(view(R1, 0, 8192), NB)
        ya_hi = v3(view(R1, 0, 4096, F16), KD)
        ya_lo = v3(view(R1, 4096, 4096, F16), KD)
        yb_hi = v3(view(R2, 0, 4096, F16), KD)
        yb_lo = v3(view(R2, 4096, 4096, F16), KD)
        x2 = v3(view(R2, 0, 8192), NB)
        mod = view(R3, 0, 6144)
        crep = v3(view(R3, 6144, 1024), KD)
        mixb = v3(view(R3, 0, 8192), GROUPS)
        m_hi = v3(view(R3, 0, 4096, F16), KD)
        m_lo = v3(view(R3, 4096, 4096, F16), KD)
        evA = v3(view(R3, 8192, 2052), 2)
        evB = v3(view(R3, 10244, 2048), 2)
        evC = v3(view(R3, 12292, 2048), 2)
        evAd = evA[:, :, 2:2 + S]
        cond_ring = v3(view(R2, 0, 8192), 4)
        diag = view(R3, 12292, 2048).rearrange("p (a b) -> p a b", b=P)
        bs_b = ring[:, 0:2, :].rearrange("p a (g i) -> p (a g) i", i=P)
        ws_t = v3(par[:, 2, :], GROUPS)
        qb = [v3(view(R2, 2048 * i, 2048), 2) for i in range(2)]
        sc = [view(R2, 4096 + 2048 * i, 2048).rearrange("p (b h k) -> p b h k", b=NB, h=2) for i in range(2)]
        keys_sb = par[:, 0:2, :].rearrange("p a (g k) -> p (a g) k", k=NKEYS)
        sc2 = view(R3, 0, 2048).rearrange("p (b h k) -> p b h k", b=NB, h=2)
        cand = view(R3, 2048, 2048).rearrange("p (b i j) -> p b i j", b=NB, i=TOPK)
        cand2 = v3(view(R3, 4096, 2048), NB)
        cmp_t = v3(view(R3, 6144, 2048), NB * TOPK)
        vals = view(R3, 8192, 256).rearrange("p (b h k) -> p b h k", b=NB, h=2)
        idx = view(R3, 8448, 256, U32).rearrange("p (b h k) -> p b h k", b=NB, h=2)
        idxf = view(R3, 8704, 256).rearrange("p (b h k) -> p b h k", b=NB, h=2)
        sel = v3(view(R3, 8960, 128, U32), NB)
        sel_a = view(R3, 9088, 128, U32)
        sel_b = view(R3, 9216, 128, U32)
        sel_af = view(R3, 9344, 128)
        sel_bf = view(R3, 9472, 128)
        tops = v3(view(R3, 9600, 128), NB)
        rsum = view(R3, 9728, 64)
        rinv = view(R3, 9792, 64)
        i1_all = view(R3, 10244, 1024).rearrange("p (b h k) -> p b h k", b=NB, h=HEADS)
        i2_all = view(R3, 11268, 1024).rearrange("p (b h k) -> p b h k", b=NB, h=HEADS)
        s_all = view(R3, 12292, 1024).rearrange("p (b h k) -> p b h k", b=NB, h=HEADS)
        keys_t16 = v3(view(R3, 0, 1024, F16), 2)
        gates16 = v3(view(R3, 1024, 1024, F16), 2)
        g_t = view(R3, 2048, 1024)
        iota_k4 = v3(view(R3, 3072, 256, F16), P)
        oh_keys = view(R3, 3328, 4 * 512, F16).rearrange("p (r c k t) -> p r c k t", r=4, c=2, t=4)
        oh_gate = view(R3, 5376, 4 * 512, F16).rearrange("p (r c k t) -> p r c k t", r=4, c=2, t=4)
        gbuf = [view(*at, 4096).rearrange("p (k t) -> p k t", t=32) for at in ((R2, 0), (R3, 7424))]
        h2_sp = v3(view(R2, 6144, 2048), NSP)
        rows = [par[:, 0, :], par[:, 1, :], par[:, 2, :], view(R3, 12800, 1024)]
        idx_sp = view(R3, 13824, SLOTS, U32)
        gate_sp = view(R3, 13824 + SLOTS, SLOTS)
        A_t = v3(view(R2, 0, 4 * DT), 4)
        G_t = view(R2, 4 * DT, 4 * DT).rearrange("p (n j t) -> p n j t", n=DT // 32, j=4)
        c_hi = [v3(view(R3, 0, 2 * DT, F16), 4), v3(view(R3, 4 * DT + NB * D, 2 * DT, F16), 4)]
        c_lo = [v3(view(R3, 2 * DT, 2 * DT, F16), 4),
                ring[:, :, :].rearrange("p a b -> p (a b)").bitcast(F16)[:, 0:4 * DT].rearrange("p (a b) -> p a b", a=4)]
        acc = v3(view(R3, 4 * DT, NB * D), NB)
        par_end = v3(view(R2, 0, 3 * D), 3)

        psU = [ctx.enter_context(nc.psum_tensor(f"psU{i}", [P, 512], F32)) for i in range(4)]
        psX = [ctx.enter_context(nc.psum_tensor(f"psX{i}", [P, 512], F32)) for i in range(4)]

        a_dram = nc.dram_tensor("a_dram", [EARLY, P, 4, DT], F32).ap()
        mod_dram = nc.dram_tensor("mod_dram", [1, 6 * D], F32).ap()
        g_dram = nc.dram_tensor("g_dram", [NGRP, P, DT // 32, P], F32).ap()

        consts_in = sem("consts_in")
        x_in = sem("x_in")
        stage_in = [sem("stage_in0"), sem("stage_in1")]
        mod_stored = sem("mod_stored")
        par_in = sem("par_in")
        x2_in = sem("x2_in")
        keys_in = sem("keys_in")
        g_stored = [sem("g_stored0"), sem("g_stored1")]
        g_in = sem("g_in")
        bs_in = sem("bs_in")
        b_cond_in = [sem("b_cond_in0"), sem("b_cond_in1")]
        cond_in = [sem(f"cond_in{r}") for r in range(4)]
        a_stored = [sem(f"a_stored{r}") for r in range(4)]
        a_in = sem("a_in")
        out_stored = sem("out_stored")
        zeroed = sem("zeroed")
        ident_ready = sem("ident_ready")
        tanh_c = sem("tanh_c")
        crep_ready = sem("crep_ready")
        mask_ready = sem("mask_ready")
        var_ready = sem("var_ready")
        std_ready = sem("std_ready")
        norm_ready = sem("norm_ready")
        th_ready = sem("th_ready")
        h_split = sem("h_split")
        y_norm = sem("y_norm")
        rows_in = sem("rows_in")
        slots_ready = sem("slots_ready")
        h2_ready = sem("h2_ready")
        idx_step = sem("idx_step")
        row_in = [sem(f"row_in{i}") for i in range(4)]
        row_used = sem("row_used")
        acc_zeroed = sem("acc_zeroed")
        window_set = sem("window_set")
        carried = sem("carried")
        gelu_ready = sem("gelu_ready")
        weight_ready = sem("weight_ready")
        pool_step = sem("pool_step")
        hi_done = sem("hi_done")
        lo_done = sem("lo_done")
        tile_ready = sem("tile_ready")
        tile_free = sem("tile_free")
        aux_ready = sem("aux_ready")
        aux_free = sem("aux_free")
        act_ready = sem("act_ready")
        ev_free = sem("ev_free")
        x1_ready = sem("x1_ready")
        sc_ready = sem("sc_ready")
        sc_free = sem("sc_free")
        sc_used = sem("sc_used")
        s_shift = sem("s_shift")
        s_exp = sem("s_exp")
        gate_ready = sem("gate_ready")
        oh_keys_ready = sem("oh_keys_ready")
        oh_ready = sem("oh_ready")
        g_ready = sem("g_ready")
        g_free = sem("g_free")
        a_free = sem("a_free")
        g_used = sem("g_used")
        v_ready = sem("v_ready")
        v_free = sem("v_free")
        y_ready = sem("y_ready")
        dve_step = sem("dve_step")

        block = ctx.enter_context(nc.Block())

        def wait(eng, s, value):
            if not isinstance(value, int) or value > 0:
                eng.wait_ge(s, value)

        def front_units(rows):
            return w_front[rows].rearrange("p k n -> p (k n)")

        @block.sync
        def _(sp):
            sp.dma_start(ccol[:, :], c_col).then_inc(consts_in, 16)
            for u in range(2):
                sp.dma_start(stage[:, u, :], w_cond[u]).then_inc(stage_in[u], 16)
            sp.dma_start(xt, x.rearrange("(b p) d -> p b d", p=P)).then_inc(x_in, 16)
            sp.dma_start(mod[:, 0:2 * D], b_cond[0:2 * D].partition_broadcast(P)).then_inc(b_cond_in[0], 16)
            with sp.Fori(1, COND1 // 2) as i:
                for u in range(2):
                    sp.wait_ge(aux_ready, i * 2 + (u - 1))
                    sp.dma_start(stage[:, u, :], w_cond[i * 2 + u]).then_inc(stage_in[u], 16)
            for u in range(2):
                sp.wait_ge(aux_ready, COND1 - 1 + u)
                sp.dma_start(stage[:, u, :], front_units(u)).then_inc(stage_in[u], 16)
            for r in range(4):
                sp.dma_start(cond_ring[:, r, :], w_cond[COND1 + r]).then_inc(cond_in[r], 16)
            sp.dma_start(mod[:, 2 * D:6 * D], b_cond[2 * D:6 * D].partition_broadcast(P)).then_inc(b_cond_in[1], 16)
            sp.dma_start(cw[:, :, :], conv_w).then_inc(consts_in, 16)
            sp.dma_start(par[:, 0, :], ln_g.partition_broadcast(P)).then_inc(consts_in, 16)
            sp.dma_start(par[:, 1, :], ln_b.partition_broadcast(P)).then_inc(consts_in, 16)
            sp.dma_start(ws_t, w_spat).then_inc(consts_in, 16)
            sp.wait_ge(h_split, 16)
            sp.dma_start(bs_b.rearrange("p g i -> p (g i)"), b_spat.partition_broadcast(P)).then_inc(bs_in, 16)

            def load_front(n, u):
                sp.wait_ge(lo_done, n - 1)
                sp.dma_start(stage[:, u, :], front_units(n)).then_inc(stage_in[u], 16)

            def load_pairs(first, last):
                with sp.Fori(first // 2, last // 2) as i:
                    for u in range(2):
                        load_front(i * 2 + u, u)

            for v in range(N_V):
                load_front(v + 2, v % 2)
                if v + 1 < N_V:
                    for r in range(4):
                        sp.wait_ge(aux_ready, A_COND2 + 4 * v + r + 1)
                        sp.dma_start(cond_ring[:, r, :], w_cond[COND1 + 4 * (v + 1) + r]).then_inc(cond_in[r], 16)
            sp.wait_ge(aux_free, A_MIX)
            sp.dma_start(mod_dram, mod[0:1, :]).then_inc(mod_stored, 16)
            load_pairs(U_CONV + 2, U_O + 2)
            sp.wait_ge(tile_ready, T_O - 4)
            sp.wait_ge(mod_stored, 16)
            sp.dma_start(par[:, 0, :], mod_dram[0, 2 * D:3 * D].partition_broadcast(P)).then_inc(par_in, 16)
            sp.dma_start(x2, x.rearrange("(b p) d -> p b d", p=P)).then_inc(x2_in, 16)
            sp.dma_start(par[:, 1, :], ln1_g.partition_broadcast(P)).then_inc(par_in, 16)
            sp.dma_start(par[:, 2, :], ln1_b.partition_broadcast(P)).then_inc(par_in, 16)
            load_pairs(U_O + 2, U_O + 4)

            def load_u(n, e, p):
                sp.wait_ge(lo_done, n - 1)
                sp.dma_start(stage[:, p, :], u_units[e]).then_inc(stage_in[p], 16)

            def load_v(n, g, half):
                sp.wait_ge(lo_done, n - 1)
                sp.dma_start(stage[:, half, :].rearrange("p (j d) -> p j d", j=4),
                             expert_v[g][:, :, half * HT:half * HT + HT]).then_inc(stage_in[half], 16)

            def load_q(n, h):
                sp.wait_ge(lo_done, n - 1)
                sp.dma_start(stage[:, 0, :], front_units(h + U_Q)).then_inc(stage_in[0], 16)

            def load_gates(g):
                sp.dma_start(G_t, g_dram[g].rearrange("p n (j t) -> p n j t", j=4)).then_inc(g_in, 16)

            load_q(U_Q, 0)
            load_u(U_Q + 1, 0, 1)
            sp.wait_ge(x1_ready, 1)
            sp.dma_start(keys_sb, keys_t).then_inc(keys_in, 16)

            def load_head_pair(i, first):
                for q in range(2):
                    if first + q:
                        sp.wait_ge(lo_done, i * 6 + (U_Q + 3 * q - 1))
                        sp.dma_start(stage[:, q, :], front_units(i * 2 + (U_Q + q))).then_inc(stage_in[q], 16)
                    for e in range(2):
                        if first + q + e:
                            load_u(i * 6 + (U_Q + 3 * q + 1 + e), i * 4 + (2 * q + e), (q + 1 + e) % 2)

            load_head_pair(0, 0)
            with sp.Fori(1, HEADS // 2) as i:
                load_head_pair(i, 1)
            for k in range(N_TAIL - 1):
                load_u(U_TAIL + k, N_HEAD + k, k % 2)
            sp.wait_ge(sc_ready, 4 * HEADS)
            for k in range(2):
                sp.dma_start(par[:, k, :], mod_dram[0, (3 + k) * D:(4 + k) * D].partition_broadcast(P)).then_inc(rows_in, 16)
            for k in range(N_TAIL - 1, N_TAIL + 3):
                load_u(U_TAIL + k, N_HEAD + k, k % 2)

            def spread_unit(b4, n, load):
                for b in range(2):
                    sp.wait_ge(g_free, b4 * 8 + 8 * (b + 1))
                    sp.dma_start(g_dram[:, :, b4 + b, :].rearrange("g p n -> p g n"),
                                 gbuf[b].rearrange("p (g j) t -> p g (j t)", g=NGRP)).then_inc(g_stored[b], 16)
                load(n)

            with sp.Fori(0, N_SPREAD // 2 - 1) as i:
                for u in range(2):
                    spread_unit(i * 4 + 2 * u, i * 2 + (U_SPREAD + 3 + u),
                                lambda n: load_u(n, i * 2 + (N_HEAD + N_TAIL + 3 + u), (1 + u) % 2))
            spread_unit(2 * N_SPREAD - 4, U_VE - 3, lambda n: load_u(n, 2 * EARLY - 3, 1))
            spread_unit(2 * N_SPREAD - 2, U_VE - 2, lambda n: load_u(n, 2 * EARLY - 2, 0))
            for b in range(2):
                sp.wait_ge(g_stored[b], 16 * N_SPREAD)
            for r in range(4):
                sp.wait_ge(a_stored[r], 16 * 2)
            sp.dma_start(A_t, a_dram[0]).then_inc(a_in, 16)
            load_gates(0)
            load_u(U_VE - 1, 2 * EARLY - 1, 1)
            load_v(U_VE, 0, 0)
            load_v(U_VE + 1, 0, 1)
            load_v(U_VE + 2, 1, 0)
            for r in range(4):
                sp.wait_ge(a_stored[r], 16 * 2 * EARLY)

            def next_early(c):
                sp.wait_ge(a_free, c + 1)
                sp.dma_start(A_t, a_dram[c + 1]).then_inc(a_in, 16)
                sp.wait_ge(g_used, c + 1)
                load_gates(c + 1)
                load_v(c * 2 + (U_VE + 3), c + 1, 1)

            with sp.Fori(0, EARLY - 2) as c:
                next_early(c)
                load_v(c * 2 + (U_VE + 4), c + 2, 0)
            next_early(EARLY - 2)
            load_u(U_LATE, 2 * EARLY, 0)
            sp.wait_ge(g_used, EARLY)
            load_gates(EARLY)
            load_u(U_LATE + 1, 2 * EARLY + 1, 1)
            with sp.Fori(0, NGRP - 1 - EARLY) as i:
                for half in range(2):
                    load_u(i * 4 + (U_LATE + 2 + half), i * 2 + (2 * EARLY + 2 + half), half)
                for half in range(2):
                    load_v(i * 4 + (U_LATE + 4 + half), i + EARLY, half)
                sp.wait_ge(g_used, i + (EARLY + 1))
                load_gates(i + (EARLY + 1))
            for half in range(2):
                load_v(U_LAST + half, NGRP - 1, half)
            sp.wait_ge(a_free, NGRP)
            sp.dma_start(par_end[:, 0, :], mod_dram[0, 5 * D:6 * D].partition_broadcast(P)).then_inc(par_in, 16)
            sp.dma_start(par_end[:, 1, :], ln2_g.partition_broadcast(P)).then_inc(par_in, 16)
            sp.dma_start(par_end[:, 2, :], ln2_b.partition_broadcast(P)).then_inc(par_in, 16)
            for n, b in enumerate(END_ORDER):
                sp.wait_ge(y_ready, n + 1)
                sp.dma_start(out[b * P:(b + 1) * P, :], xt[:, b, :]).then_inc(out_stored, 16)
            sp.wait_ge(out_stored, 16 * NB)

        @block.gpsimd
        def _(pool):
            pool.memset(ident[:, :], 0.0).then_inc(zeroed, 1)
            pool.wait_ge(zeroed, 1)
            pool.affine_select(out=ident[:, :], in_=ident[:, :], compare_op=ALU.not_equal, fill=1.0, base=0,
                               pattern=[[-1, P]], channel_multiplier=1).then_inc(ident_ready, 1)
            pool.iota(iota_i[:, :], pattern=[[1, P]], base=0, channel_multiplier=0).then_inc(ident_ready, 1)
            pool.wait_ge(consts_in, 16 * 5)
            pool.wait_ge(ident_ready, 2)
            pool.memset(ws_t[64:P, :, 0:64], 0.0).then_inc(mask_ready, 1)

            def store_acts(t, g, half):
                for r in range(4):
                    pool.wait_ge(tile_free, t + (r + 1))
                    pool.dma_start(a_dram[g, :, 2 * half + r // 2, (r % 2) * HD:(r % 2 + 1) * HD],
                                   ring[:, r, 0:HD]).then_inc(a_stored[r], 16)

            with pool.Fori(0, HEADS) as h:
                for half in range(2):
                    store_acts(h * 12 + (T_Q + 4 * half + 4), h, half)
            with pool.Fori(0, (N_TAIL + N_SPREAD) // 2) as i:
                for half in range(2):
                    store_acts(i * 8 + (T_TAIL + 4 * half), i + HEADS, half)

            def window(n, p, slot, size, used):
                wait(pool, row_used, used)
                pool.tensor_copy(idx_now[:, p, 0:size], idx_sp[:, slot]).then_inc(idx_step, 1)
                pool.wait_ge(idx_step, n)
                if not isinstance(n, int) or n > 1:
                    pool.wait_ge(window_set, n - 1)
                pool.tensor_tensor(carrier[:, 0:1], ident[:, 0:1], ident[:, 0:1], ALU.add).then_inc(window_set, 1)

            def gather(table, p, at, m, r, first=False):
                if not first:
                    pool.wait_ge(row_used, m - 3)
                    if not isinstance(m, int) or m > 4:
                        pool.wait_ge(carried, m - 4)
                    pool.tensor_tensor(carrier[:, 1:2], ident[:, 0:1], ident[:, 0:1], ALU.add).then_inc(carried, 1)
                pool.indirect_dma_start(rows[r], None, table,
                                        bass.IndirectOffsetOnAxis(ap=idx_now[:, p, at:at + 1], axis=0)).then_inc(row_in[r], 16)

            def section(k, c, p, slot, m, mc, before):
                window(c + 2, p, slot, k + LAG, m - before)
                for j in range(k):
                    gather(u_rows, p, LAG + j, m + j, (mc + j) % 4)
                for j in range(k):
                    gather(v_rows, p, j, m + (k + j), (mc + k + j) % 4)

            pool.wait_ge(slots_ready, 1)
            pool.wait_ge(h2_ready, 1)
            window(1, 1, slice(0, LAG), LAG, 0)
            for j in range(4):
                gather(u_rows, 1, j, j, j, True)
            pool.wait_ge(g_ready, DT // 4)
            pool.wait_ge(g_stored[1], 16 * N_SPREAD)
            pool.memset(R3[:, 4 * DT:4 * DT + NB * D], 0.0).then_inc(acc_zeroed, 1)
            for n in range(N_POST):
                store_acts(T_POST + 4 * n, EARLY - N_POST // 2 + n // 2, n % 2)
                for j in range(4 + 6 * n, min(10 + 6 * n, LAG)):
                    gather(u_rows, 1, j, j, j % 4)
            with pool.Fori(0, (EARLY - 1) // 2) as i:
                for k in range(2):
                    mc = LAG + 2 * K_EARLY * k
                    section(K_EARLY, i * 2 + k, k, bass.ds(i * 2 * K_EARLY + K_EARLY * k, K_EARLY + LAG),
                            i * 4 * K_EARLY + mc, mc, LAG)
            mc = LAG + 2 * S_GAP
            section(K_GAP, EARLY - 1, (EARLY - 1) % 2, slice(S_GAP, S_GAP + K_GAP + LAG), mc, mc, 2 * K_EARLY)
            with pool.Fori(0, (NGRP - 1 - EARLY) // 2) as i:
                for k in range(2):
                    mc = LAG + 2 * S_LATE + 2 * K_LATE * k
                    section(K_LATE, i * 2 + (EARLY + k), (EARLY + k) % 2,
                            bass.ds(i * 2 * K_LATE + (S_LATE + K_LATE * k), K_LATE + LAG),
                            i * 4 * K_LATE + mc, mc, 2 * K_GAP if K_GAP < K_LATE else 2 * K_LATE)
            window(NGRP + 1, (NGRP - 1) % 2, slice(SLOTS - LAG, SLOTS), LAG, 2 * SLOTS - LAG - 2 * K_LATE)
            for j in range(LAG):
                gather(v_rows, (NGRP - 1) % 2, j, 2 * SLOTS - LAG + j, j % 4)
            for n, b in enumerate(END_ORDER):
                pool.wait_ge(y_norm, n + 1)
                pool.tensor_tensor(xt[:, b, :], xt[:, b, :], par_end[:, 1, :], ALU.mult).then_inc(pool_step, 1)
                pool.wait_ge(pool_step, n + 1)
                pool.tensor_tensor(xt[:, b, :], xt[:, b, :], par_end[:, 2, :], ALU.add).then_inc(y_ready, 1)

        @block.scalar
        def _(act):
            def make_hi(p, pair):
                act.wait_ge(stage_in[p], pair * 16 + 16 * (COND1 // 2 + 1))
                nc.scalar.activation(w_hi[:, p, :], stage[:, p, :], ACT.Copy, scale=WS).then_inc(hi_done, 1)

            def evacuate(t, dst, src, func=ACT.Copy, scale=DESCALE):
                act.wait_ge(tile_ready, t + 1)
                nc.scalar.activation(dst, src, func, scale=scale).then_inc(tile_free, 1)

            def root(k, blocks=slice(0, NB)):
                act.wait_ge(var_ready, k + 1)
                nc.scalar.activation(std[:, blocks], vare[:, blocks], ACT.Sqrt).then_inc(std_ready, 1)

            def feature_unit(t, dst, func=ACT.Copy, scale=DESCALE):
                for j in range(2):
                    for half in range(2):
                        evacuate(t + (2 * j + half), dst[:, j, half * HT:(half + 1) * HT],
                                 psU[2 * j + half][:, :], func, scale)

            def h_hi_tiles(first, done):
                for a in range(16):
                    k, half = a % 8, a // 8
                    act.wait_ge(aux_free, first + a + 1)
                    nc.scalar.activation(h_hi[:, k, half * HT:(half + 1) * HT], ring[:, a % 4, :],
                                         ACT.Copy).then_inc(th_ready, 1)

            act.wait_ge(consts_in, 16)
            nc.scalar.activation(cth[:, :], ccol[:, :], ACT.Tanh, scale=0.5).then_inc(tanh_c, 1)
            root(0)
            h_hi_tiles(A_HT, 0)
            for p in range(2):
                make_hi(p, 0)
            for u in range(N_V):
                for b in range(NB):
                    evacuate(T_V + 8 * u + b, xt[:, b, u * UC:(u + 1) * UC], psU[b % 4][:, 0:UC], ACT.Gelu_apprx_tanh)
                make_hi(u % 2, (u + 2) // 2)
            root(1)
            with act.Fori(0, 2) as i:
                for q in range(2):
                    for r, dst in enumerate((evAd, evB, evB)):
                        m = 3 * q + r
                        act.wait_ge(ev_free, i * 4 + (E_CONV + 2 * q + r // 2))
                        feature_unit(i * 24 + (T_CONV + 4 * m), dst)
                        make_hi(m % 2, i * 3 + (U_CONV + m + 2) // 2)
            for j in range(N_U):
                act.wait_ge(ev_free, E_U + max(0, j - 1))
                feature_unit(T_U + 4 * j, (evAd, evB)[j % 2], ACT.Gelu_apprx_tanh)
                make_hi(j % 2, (U_U + j + 2) // 2)
            with act.Fori(0, 4) as i:
                for r, dst in enumerate((evAd, evB, evC, evB)):
                    act.wait_ge(ev_free, i * 2 + (E_MERGE + r // 3))
                    if r % 2:
                        feature_unit(i * 16 + (T_MERGE + 4 * r), dst, ACT.Tanh, 0.5 * DESCALE)
                    else:
                        feature_unit(i * 16 + (T_MERGE + 4 * r), dst)
                    make_hi(r % 2, i * 2 + (U_MERGE + r + 2) // 2)
            for u in range(N_O):
                for b in range(NB):
                    evacuate(T_O + 8 * u + b, xt[:, b, u * UC:(u + 1) * UC], psU[b % 4][:, 0:UC])
                make_hi(u % 2, (U_O + u + 2) // 2)
            root(2)
            root(3, slice(0, 4))
            root(4, slice(4, 8))
            h_hi_tiles(A_H2T, 16)

            def early_acts(t, e):
                for r in range(4):
                    wait(act, a_stored[r], e * 16)
                    evacuate(t + r, ring[:, r, 0:HD], psU[r][:, 0:HD], ACT.Gelu_apprx_tanh)

            def heads(i):
                for q in range(2):
                    t = i * 24 + (T_Q + 12 * q)
                    n = 3 * q + U_Q + 2

                    def next_hi(r):
                        make_hi((n + r) % 2, i * 3 + (n + r) // 2)

                    wait(act, sc_ready, i * 8 + 4 * (q - 1))
                    feature_unit(t, qb[q])
                    next_hi(0)
                    wait(act, sc_used, i * 2 + (q - 1))
                    for b in range(4):
                        act.wait_ge(sc_ready, i * 8 + (4 * q + b + 1))
                        nc.scalar.activation(sc[q][:, 2 * b:2 * b + 2, :, :].rearrange("p b h k -> p (b h k)"),
                                             psX[b][:, :], ACT.Copy).then_inc(sc_free, 1)
                    for e in range(2):
                        early_acts(t + (4 + 4 * e), i * 4 + (2 * q + e))
                        next_hi(1 + e)

            heads(0)
            with act.Fori(1, HEADS // 2) as i:
                heads(i)
            for k in range(2):
                early_acts(T_TAIL + 4 * k, N_HEAD + k)
                make_hi(k, (U_TAIL + 2) // 2)
            act.wait_ge(s_shift, 1)
            s_flat = s_all.rearrange("p b h k -> p (b h k)")
            nc.scalar.activation(s_flat, s_flat, ACT.Exp).then_inc(s_exp, 1)
            for k in range(2, N_TAIL):
                early_acts(T_TAIL + 4 * k, N_HEAD + k)
                make_hi(k % 2, (U_TAIL + k + 2) // 2)

            def collect(i):
                for u in range(2):
                    e = i * 2 + (N_HEAD + N_TAIL + u)
                    for r in range(4):
                        b = r // 2
                        if r % 2 == 0:
                            wait(act, g_stored[b], i * 32 + 16 * u)
                        for q in range(4):
                            act.wait_ge(g_ready, i * 32 + (16 * u + 4 * r + q + 1))
                            at = 16 * (r % 2) + 4 * q
                            nc.scalar.activation(gbuf[b][:, :, at:at + 4],
                                                 psX[q][:, :].rearrange("p (t k) -> p k t", t=4),
                                                 ACT.Copy, scale=1.0 / GS).then_inc(g_free, 1)
                        wait(act, a_stored[r], e * 16)
                        evacuate(i * 8 + (T_SPREAD + 4 * u + r), ring[:, r, 0:HD], psU[r][:, 0:HD], ACT.Gelu_apprx_tanh)
                    make_hi(u, i + (U_SPREAD + 2) // 2)

            collect(0)
            with act.Fori(1, N_SPREAD // 2) as i:
                collect(i)

            def gelu_dots(n, m, k):
                act.wait_ge(row_used, m)
                nc.scalar.activation(dots[:, 0:k], dots[:, 0:k], ACT.Gelu_apprx_tanh).then_inc(gelu_ready, 1)

            for k in range(N_POST):
                early_acts(T_POST + 4 * k, N_HEAD + N_TAIL + N_SPREAD + k)
                make_hi(k % 2, (U_POST + 2 + k) // 2)
                if k == 1:
                    gelu_dots(0, LAG, LAG)

            def after_v(c, pair, m, k):
                for half in range(2):
                    act.wait_ge(v_ready, c * VT + DB * (half + 1))
                    make_hi(half, pair)
                gelu_dots(c, m, k)

            def late_acts(t, g, pair):
                act.wait_ge(a_free, g)
                for half in range(2):
                    for j in range(2):
                        for r in range(2):
                            evacuate(t + (4 * half + 2 * j + r), A_t[:, 2 * half + j, r * HD:(r + 1) * HD],
                                     psU[2 * j + r][:, 0:HD], ACT.Gelu_apprx_tanh)
                    make_hi(half, pair)

            with act.Fori(0, EARLY - 1) as c:
                after_v(c, c + (U_VE + 2) // 2, c * 2 * K_EARLY + (LAG + K_EARLY), K_EARLY)
            after_v(EARLY - 1, U_LATE // 2, LAG + 2 * S_GAP + K_GAP, K_GAP)
            late_acts(T_LATE, EARLY, (U_LATE + 2) // 2)
            with act.Fori(0, NGRP - 1 - EARLY) as i:
                late_acts(i * 8 + (T_LATE + 8), i + (EARLY + 1), i * 2 + (U_LATE + 4) // 2)
                after_v(i + EARLY, i * 2 + (U_LATE + 6) // 2, i * 2 * K_LATE + (LAG + 2 * S_LATE + K_LATE), K_LATE)
            for n, b in enumerate(END_ORDER):
                root(5 + n, slice(b, b + 1))

        @block.vector
        def _(dve):
            V = nc.vector
            count = [0]
            base = [0]

            def step(ins):
                count[0] += 1
                return ins.then_inc(dve_step, 1)

            def settle():
                dve.wait_ge(dve_step, base[0] + count[0])

            def repeat(first, last, steps, body):
                start = count[0]
                with dve.Fori(first, last) as i:
                    base[0] = i * steps + (start - first * steps)
                    count[0] = 0
                    body(i)
                    assert count[0] == steps, (body, count[0])
                base[0] = 0
                count[0] = start + steps * (last - first)

            def make_lo(n, p):
                dve.wait_ge(hi_done, n + 1)
                V.scalar_tensor_tensor(w_lo[:, p, :], stage[:, p, :], WS, w_hi[:, p, :],
                                       ALU.mult, ALU.subtract).then_inc(lo_done, 1)

            def split(hi, lo, src, scale, done):
                step(V.tensor_scalar(hi, src, scale, None, ALU.mult))
                settle()
                V.scalar_tensor_tensor(lo, src, scale, hi, ALU.mult, ALU.subtract).then_inc(done, 1)

            def statistics(src, blocks=range(NB)):
                for b in blocks:
                    for half in range(2):
                        step(V.bn_stats(stats[:, b, half, :], src[:, b, half * HT:(half + 1) * HT]))
                settle()
                aggregate(blocks, 2)

            def aggregate(blocks, parts):
                for b in blocks:
                    step(V.bn_aggr(mv[:, b, :], stats[:, b, 0:parts, :]))
                settle()
                at = slice(blocks[0], blocks[-1] + 1)
                V.tensor_scalar(vare[:, at], mv[:, at, 1], EPS, None, ALU.add).then_inc(var_ready, 1)

            def normalise(k, dst, src, done, blocks=range(NB)):
                dve.wait_ge(std_ready, k + 1)
                at = slice(blocks[0], blocks[-1] + 1)
                step(V.reciprocal(rstd[:, at], std[:, at]))
                settle()
                for b in blocks:
                    ins = V.tensor_scalar(dst[:, b, :], src[:, b, :], mv[:, b, 0:1], rstd[:, b:b + 1],
                                          ALU.subtract, ALU.mult)
                    if done is None or b != blocks[-1]:
                        step(ins)
                    else:
                        ins.then_inc(done, 1)

            def row(ap, blocks=NB):
                return ap.unsqueeze(1).to_broadcast([P, blocks, ap.shape[1]])

            def split_h(first, before, shift, scale):
                for a in range(16 + 2):
                    if a < 16:
                        k = a % 8
                        dve.wait_ge(aux_ready, first + a + 1)
                        wait(dve, h_split, before + a - 3 if a >= 4 else 0)
                        V.tensor_scalar(ring[:, a % 4, :], psX[a % 4][:, :], cols[:, scale, k:k + 1],
                                        cols[:, shift, k:k + 1], ALU.mult, ALU.add).then_inc(aux_free, 1)
                    if a >= 2:
                        k, half = (a - 2) % 8, (a - 2) // 8
                        dve.wait_ge(th_ready, before + a - 1)
                        at = slice(half * HT, (half + 1) * HT)
                        V.tensor_tensor(h_lo[:, k, at], ring[:, (a - 2) % 4, :], h_hi[:, k, at],
                                        ALU.subtract).then_inc(h_split, 1)

            def columns(kind, start):
                settle()
                step(V.tensor_tensor(diag, mod[:, start * D:(start + 2) * D].rearrange("p (a b) -> p a b", b=P),
                                     ident[:, :].unsqueeze(1).to_broadcast([P, 2 * KD, P]), ALU.mult))
                settle()
                step(V.tensor_reduce(cols[:, kind:kind + 2, :].rearrange("p a k -> p (a k)"), diag, AX_X, ALU.add))
                settle()
                step(V.tensor_scalar(cols[:, kind, :], cols[:, kind, :], AS, None, ALU.mult))
                step(V.tensor_scalar(cols[:, kind + 1, :], cols[:, kind + 1, :], 1.0, AS, ALU.add, ALU.mult))
                settle()

            def cond_rows(u, a):
                dve.wait_ge(aux_ready, a + 1)
                part = mod[:, u * UC:(u + 1) * UC]
                V.tensor_tensor(part, psX[a % 4][:, 0:UC], part, ALU.add).then_inc(aux_free, 1)

            dve.wait_ge(ident_ready, 2)
            step(V.tensor_copy(iota_f[:, :], iota_i[:, 0:TOPK]))
            V.memset(evA[:, :, 0:2], 0.0).then_inc(ev_free, 1)
            dve.wait_ge(tanh_c, 1)
            step(V.tensor_scalar(cth[:, :], cth[:, :], 1.0, 0.5, ALU.add, ALU.mult))
            settle()
            step(V.tensor_tensor(cth[:, :], cth[:, :], ccol[:, :], ALU.mult))
            settle()
            V.tensor_copy(crep, cth[:, :].unsqueeze(2).to_broadcast([P, KD, P])).then_inc(crep_ready, 1)
            dve.wait_ge(x_in, 16)
            statistics(xt)
            normalise(0, xt, xt, norm_ready)
            dve.wait_ge(b_cond_in[0], 16)
            for u in range(COND1):
                cond_rows(u, u)
            dve.wait_ge(aux_free, COND1)
            columns(0, 0)
            split_h(A_HT, 0, 0, 1)
            make_lo(0, 0)
            make_lo(1, 1)
            dve.wait_ge(b_cond_in[1], 16)
            for v in range(N_V):
                dve.wait_ge(tile_free, T_V + 8 * (v + 1))
                make_lo(v + 2, v % 2)
                for r in range(4):
                    cond_rows(COND1 + 4 * v + r, A_COND2 + 4 * v + r)
            dve.wait_ge(aux_free, A_MIX)
            statistics(xt)
            normalise(1, xt, xt, None)
            settle()
            step(V.tensor_tensor(xt, xt, row(par[:, 0, :]), ALU.mult))
            settle()
            V.tensor_tensor(xt, xt, row(par[:, 1, :]), ALU.add).then_inc(norm_ready, 1)
            columns(2, 3)

            def conv(i):
                for q in range(2):
                    qc = i * 4 + 2 * q
                    m = 3 * q
                    t = i * 24 + (T_CONV + 4 * m)
                    n = i * 6 + (U_CONV + m + 2)
                    make_lo(n, m % 2)
                    make_lo(n + 1, (m + 1) % 2)
                    dve.wait_ge(tile_free, t + 8)
                    V.tensor_tensor(evAd, evAd, evB, ALU.mult).then_inc(ev_free, 1)
                    dve.wait_ge(ev_free, i * 4 + (E_CONV + 2 * q + 1))

                    def weight(j, tap):
                        return cw[:, bass.ds(qc + j, 1), tap:tap + 1].rearrange("p a b -> p (a b)")

                    for j in range(2):
                        step(V.tensor_scalar(evC[:, j, :], evA[:, j, 0:S], weight(j, 0), None, ALU.mult))
                    settle()
                    for tap in (1, 2):
                        for j in range(2):
                            step(V.scalar_tensor_tensor(evC[:, j, :], evA[:, j, tap:tap + S], weight(j, tap),
                                                        evC[:, j, :], ALU.mult, ALU.add))
                        settle()
                    make_lo(n + 2, m % 2)
                    dve.wait_ge(tile_free, t + 12)
                    step(V.tensor_tensor(evC, evC, evB, ALU.mult))
                    settle()
                    split(yb_hi[:, bass.ds(qc, 2), :], yb_lo[:, bass.ds(qc, 2), :], evC, AS, ev_free)

            repeat(0, 2, 16, conv)
            dve.wait_ge(bs_in, 16)
            dve.wait_ge(mod_stored, 16)
            for a in range(16):
                g, half = a // 2, a % 2
                dve.wait_ge(aux_ready, A_MIX + a + 1)
                V.tensor_tensor(mixb[:, g, half * HT:(half + 1) * HT].rearrange("p (n i) -> p n i", n=4),
                                psX[a % 4][:, :].rearrange("p (n i) -> p n i", n=4),
                                bs_b[:, g:g + 1, :].to_broadcast([P, 4, P]), ALU.add).then_inc(aux_free, 1)
            dve.wait_ge(aux_free, A_H2T)
            for j in range(N_U):
                make_lo(U_U + j + 2, j % 2)
                dve.wait_ge(tile_free, T_U + 4 * (j + 1))
                ev = (evAd, evB)[j % 2]
                step(V.tensor_tensor(ev, ev, mixb[:, 2 * j:2 * j + 2, :], ALU.mult))
                settle()
                split(ya_hi[:, 2 * j:2 * j + 2, :], ya_lo[:, 2 * j:2 * j + 2, :], ev, AS, ev_free)

            def merge(i):
                qc = i * 2
                t = i * 16 + T_MERGE
                n = i * 4 + (U_MERGE + 2)
                make_lo(n, 0)
                make_lo(n + 1, 1)
                dve.wait_ge(tile_free, t + 8)
                V.scalar_tensor_tensor(evAd, evB, 1.0, evAd, ALU.add, ALU.mult).then_inc(ev_free, 1)
                make_lo(n + 2, 0)
                make_lo(n + 3, 1)
                dve.wait_ge(tile_free, t + 16)
                step(V.scalar_tensor_tensor(evC, evB, 1.0, evC, ALU.add, ALU.mult))
                settle()
                dve.wait_ge(ev_free, i * 2 + (E_MERGE + 1))
                step(V.tensor_tensor(evAd, evAd, evC, ALU.add))
                settle()
                split(m_hi[:, bass.ds(qc, 2), :], m_lo[:, bass.ds(qc, 2), :], evAd, 0.5 * AS, ev_free)

            repeat(0, 4, 3, merge)
            dve.wait_ge(par_in, 16 * 3)
            dve.wait_ge(x2_in, 16)
            for u in range(N_O):
                make_lo(U_O + u + 2, u % 2)
                dve.wait_ge(tile_free, T_O + 8 * (u + 1))
                at = slice(u * UC, (u + 1) * UC)
                step(V.tensor_tensor(xt[:, :, at], xt[:, :, at], row(par[:, 0, at]), ALU.mult))
                settle()
                step(V.scalar_tensor_tensor(xt[:, :, at], x2[:, :, at], ALPHA, xt[:, :, at], ALU.mult, ALU.add))
                settle()
                for b in range(NB):
                    step(V.bn_stats(stats[:, b, u, :], xt[:, b, at]))
            settle()
            aggregate(range(NB), N_O)
            normalise(2, xt, xt, None)
            settle()
            halves = (range(0, 4), range(4, 8))
            for k, blocks in enumerate(halves):
                part = xt[:, 4 * k:4 * k + 4, :]
                step(V.tensor_tensor(part, part, row(par[:, 1, :], 4), ALU.mult))
                settle()
                if k == 0:
                    step(V.tensor_tensor(part, part, row(par[:, 2, :], 4), ALU.add))
                    settle()
                else:
                    V.tensor_tensor(part, part, row(par[:, 2, :], 4), ALU.add).then_inc(x1_ready, 1)
                    dve.wait_ge(x1_ready, 1)
                statistics(xt, blocks)
            for k, blocks in enumerate(halves):
                normalise(3 + k, x2, xt, norm_ready, blocks)
            split_h(A_H2T, 16, 2, 3)

            def alone():
                V.memset(unread[:, :], 0.0)

            def best16(items):
                alone()
                for v, p, src, s in items:
                    step(V.max(v[:, 0:8], src))
                settle()
                alone()
                for v, p, src, s in items:
                    step(V.max_index(p[:, 0:8], v[:, 0:8], src))
                    step(V.match_replace(s, v[:, 0:8], src, LOWEST))
                settle()
                alone()
                for v, p, src, s in items:
                    step(V.max(v[:, 8:16], s))
                settle()
                alone()
                for v, p, src, s in items:
                    step(V.max_index(p[:, 8:16], v[:, 8:16], s))
                settle()

            def rank(i):
                for q in range(2):
                    h = i * 2 + q
                    s = sc[q]
                    make_lo(i * 6 + (U_Q + 3 * q + 2), q)
                    dve.wait_ge(sc_free, i * 8 + 4 * (q + 1))
                    best16([(vals[:, b, a, :], idx[:, b, a, :], s[:, b, a, :], sc2[:, b, a, :])
                            for b in range(NB) for a in range(2)])
                    V.tensor_copy(idxf, idx).then_inc(sc_used, 1)
                    make_lo(i * 6 + (U_Q + 3 * q + 3), (q + 1) % 2)
                    step(V.tensor_tensor(cand, vals[:, :, 0, :].unsqueeze(3).to_broadcast([P, NB, TOPK, TOPK]),
                                         vals[:, :, 1, :].unsqueeze(2).to_broadcast([P, NB, TOPK, TOPK]), ALU.add))
                    settle()
                    best16([(tops[:, b, :], sel[:, b, :], cand[:, b, :, :].rearrange("p i j -> p (i j)"),
                             cand2[:, b, :]) for b in range(NB)])
                    make_lo(i * 6 + (U_Q + 3 * q + 4), q)

                    def slot(dst):
                        return dst[:, :, bass.ds(h, 1), :].rearrange("p b h k -> p b (h k)")

                    step(V.tensor_copy(slot(s_all), tops))
                    sel_flat = sel.rearrange("p b k -> p (b k)")
                    step(V.tensor_scalar(sel_a, sel_flat, 4, None, ALU.logical_shift_right))
                    step(V.tensor_scalar(sel_b, sel_flat, 15, None, ALU.bitwise_and))
                    settle()
                    step(V.tensor_copy(sel_af, sel_a))
                    step(V.tensor_copy(sel_bf, sel_b))
                    settle()
                    dve.wait_ge(sc_used, h + 1)
                    for half, place, dst in ((0, sel_af, i1_all), (1, sel_bf, i2_all)):
                        step(V.tensor_tensor(cmp_t, place.unsqueeze(2).to_broadcast([P, NB * TOPK, TOPK]),
                                             iota_f[:, :].unsqueeze(1).to_broadcast([P, NB * TOPK, TOPK]), ALU.is_equal))
                        settle()
                        by_block = cmp_t.rearrange("p (b k) j -> p b k j", b=NB)
                        step(V.tensor_tensor(by_block, by_block,
                                             idxf[:, :, half, :].unsqueeze(2).to_broadcast([P, NB, TOPK, TOPK]), ALU.mult))
                        settle()
                        step(V.tensor_reduce(slot(dst), by_block, AX_X, ALU.add))
                        settle()

            repeat(0, HEADS // 2, 264, rank)
            s3 = s_all.rearrange("p b h k -> p (b h) k")
            rows3 = [P, NB * HEADS, TOPK]
            step(V.tensor_copy(rsum, s3[:, :, 0]))
            settle()
            V.tensor_tensor(s3, s3, rsum.unsqueeze(2).to_broadcast(rows3), ALU.subtract).then_inc(s_shift, 1)
            for k in range(2):
                make_lo(U_TAIL + 2 + k, k)
            dve.wait_ge(s_exp, 1)
            step(V.tensor_reduce(rsum, s3, AX_X, ALU.add))
            settle()
            step(V.reciprocal(rinv, rsum))
            settle()
            V.tensor_tensor(s3, s3, rinv.unsqueeze(2).to_broadcast(rows3), ALU.mult).then_inc(gate_ready, 1)
            make_lo(U_TAIL + 4, 0)
            step(V.tensor_copy(iota_k4, iota_i[:, :].unsqueeze(2).to_broadcast([P, P, 4])))
            for a in range(6):
                kind, half = a // 2, a % 2
                at = slice(half * HT, (half + 1) * HT)
                dve.wait_ge(aux_ready, A_IDX + a + 1)
                if kind < 2:
                    V.tensor_copy(keys_t16[:, kind, at], psX[a % 4][:, :]).then_inc(aux_free, 1)
                else:
                    V.tensor_scalar(g_t[:, at], psX[a % 4][:, :], GS, None, ALU.mult).then_inc(aux_free, 1)
            dve.wait_ge(gate_ready, 1)

            def by_slot(ap):
                return ap.rearrange("p (h k b) -> p b h k", h=HEADS, b=NSP)

            for b in range(NSP):
                step(V.scalar_tensor_tensor(by_slot(weight_sp)[:, b], i1_all[:, DB + b], float(NKEYS),
                                            i2_all[:, DB + b], ALU.mult, ALU.add))
                step(V.tensor_copy(by_slot(gate_sp)[:, b], s_all[:, DB + b]))
            settle()
            V.tensor_copy(idx_sp, weight_sp[:, :]).then_inc(slots_ready, 1)
            dve.wait_ge(rows_in, 32)
            step(V.tensor_scalar(par[:, 1, :], par[:, 1, :], 1.0, None, ALU.add))
            for b in range(NSP):
                step(V.tensor_scalar(h2_sp[:, b, :], xt[:, DB + b, :], mv[:, DB + b, 0:1],
                                     rstd[:, DB + b:DB + b + 1], ALU.subtract, ALU.mult))
            settle()
            step(V.tensor_tensor(h2_sp, h2_sp, row(par[:, 1, :], NSP), ALU.mult))
            settle()
            V.tensor_tensor(h2_sp, h2_sp, row(par[:, 0, :], NSP), ALU.add).then_inc(h2_ready, 1)
            make_lo(U_TAIL + 5, 1)
            dve.wait_ge(aux_free, A_END)
            step(V.tensor_copy(gates16[:, 0, :], g_t))
            settle()
            step(V.tensor_tensor(gates16[:, 1, :], g_t, gates16[:, 0, :], ALU.subtract))
            settle()
            make_lo(U_SPREAD, 0)

            def onehots(i):
                def tokens(src, u, q):
                    at = src[:, :, bass.ds(i * 128 + (64 * u + 4 * q), 4)]
                    return at.unsqueeze(2).to_broadcast([P, 2, P, 4])

                def gate(u, q):
                    dve.wait_ge(oh_keys_ready, i * 32 + (16 * u + q + 1))
                    both = oh_keys[:, q % 4, 1:2, :, :].to_broadcast([P, 2, P, 4])
                    V.tensor_tensor(oh_gate[:, q % 4, :, :, :], both, tokens(gates16, u, q), ALU.mult).then_inc(oh_ready, 1)

                for u in range(2):
                    for q in range(16):
                        if q == 4:
                            make_lo(i * 2 + (U_SPREAD + u + 1), (u + 1) % 2)
                        wait(dve, g_ready, i * 32 + (16 * u + q - 3))
                        keys = iota_k4.unsqueeze(1).to_broadcast([P, 2, P, 4])
                        V.tensor_tensor(oh_keys[:, q % 4, :, :, :], keys, tokens(keys_t16, u, q),
                                        ALU.is_equal).then_inc(oh_keys_ready, 1)
                        if q:
                            gate(u, q - 1)
                    gate(u, 15)

            onehots(0)
            with dve.Fori(1, N_SPREAD // 2) as i:
                onehots(i)
            make_lo(U_POST + 1, 1)
            make_lo(U_POST + 2, 0)

            def u_row(j, block, buffer):
                r, n = buffer
                dve.wait_ge(row_in[r], n)
                V.scalar_tensor_tensor(rows[r], rows[r], 1.0, h2_sp[:, block, :], ALU.mult, ALU.mult,
                                       accum_out=dots[:, j:j + 1]).then_inc(row_used, 1)

            def v_row(slot, m, block, buffer):
                r, n = buffer
                dve.wait_ge(row_in[r], n)
                dve.wait_ge(row_used, m - 1)
                dst = acc[:, DB + block, :]
                w = weight_sp[:, slot:slot + 1] if isinstance(slot, int) else weight_sp[:, bass.ds(slot, 1)]
                V.scalar_tensor_tensor(dst, rows[r], w, dst, ALU.mult, ALU.add).then_inc(row_used, 1)

            def weigh(n, slots, k):
                dve.wait_ge(gelu_ready, n)
                V.scalar_tensor_tensor(weight_sp[:, slots], dots[:, 0:k], WS * AS, gate_sp[:, slots],
                                       ALU.mult, ALU.mult).then_inc(weight_ready, 1)

            def sparse(i, c, k, sections, s0):
                def at(a, const):
                    return const if i is None else i * a + const
                m0 = LAG + 2 * s0
                per = 2 * k * sections

                def op(kind, j):
                    m = m0 + j + (k if kind is v_row else 0)
                    buffer = (m % 4, at(per * 4, 16 * (m // 4 + 1)))
                    first = () if j else (lambda: dve.wait_ge(weight_ready, at(sections, c + 1)),)

                    def run():
                        for f in first:
                            f()
                        if kind is u_row:
                            u_row(j, (s0 + LAG + j) % NSP, buffer)
                        else:
                            v_row(at(k * sections, s0 + j), at(per, m), (s0 + j) % NSP, buffer)
                    return run

                def end():
                    where = s0 + LAG
                    weigh(at(sections, c + 2), slice(where, where + k) if i is None else
                          bass.ds(at(k * sections, where), k), k)
                return [op(u_row, j) for j in range(k)] + [op(v_row, j) for j in range(k)], end

            dve.wait_ge(h2_ready, 1)
            for j in range(LAG):
                u_row(j, j % NSP, (j % 4, 16 * (j // 4 + 1)))
            make_lo(U_POST + 3, 1)
            weigh(1, slice(0, LAG), LAG)

            def coefficients(g, p):
                def product(j):
                    if j == 0:
                        dve.wait_ge(g_in, g * 16 + 16)
                    a = A_t[:, j, :].rearrange("p (n t) -> p n t", n=DT // 32)
                    ins = V.scalar_tensor_tensor(a, a, AS, G_t[:, :, j, :], ALU.mult, ALU.mult)
                    if j < 3:
                        step(ins)
                    else:
                        ins.then_inc(g_used, 1)

                def hi():
                    dve.wait_ge(g_used, g + 1)
                    settle()
                    step(V.tensor_scalar(c_hi[p], A_t, 1.0, None, ALU.mult))

                def lo():
                    settle()
                    V.tensor_tensor(c_lo[p], A_t, c_hi[p], ALU.subtract).then_inc(a_free, 1)

                return [lambda j=j: product(j) for j in range(4)] + [hi, lo]

            def gather_out(c, n, between=()):
                between = list(between)
                total = len(between)
                for half in range(2):
                    for b in range(DB):
                        dve.wait_ge(v_ready, c * VT + (DB * half + b + 1))
                        dst = acc[:, b, half * HT:(half + 1) * HT]
                        V.tensor_tensor(dst, psX[(DB * half + b) % 4][:, :], dst, ALU.add).then_inc(v_free, 1)
                        done = DB * half + b + 1
                        while total - len(between) < -(-total * done // VT):
                            between.pop(0)()
                    make_lo(n + half, half)

            def early(i, p):
                g = i * 2 + p

                def start():
                    dve.wait_ge(a_in, g * 16 + 32)
                pieces = coefficients(g + 1, 1 - p)
                first = pieces[0]
                pieces[0] = lambda: (start(), first())
                ops, end = sparse(i, p, K_EARLY, 2, p * K_EARLY)
                gather_out(g, i * 4 + (U_VE + 2 + 2 * p), ops[:K_EARLY] + pieces + ops[K_EARLY:])
                end()

            dve.wait_ge(g_ready, DT // 4)
            dve.wait_ge(acc_zeroed, 1)
            dve.wait_ge(a_in, 16)
            for piece in coefficients(0, 0):
                piece()
            for p in range(2):
                make_lo(U_VE + p, p)

            def early_pair(i):
                for p in range(2):
                    early(i, p)

            repeat(0, (EARLY - 1) // 2, 8, early_pair)
            ops, end = sparse(None, EARLY - 1, K_GAP, 1, S_GAP)
            gather_out(EARLY - 1, U_LATE, ops[:12])
            for op in ops[12:]:
                op()
            end()
            for p in range(2):
                make_lo(U_LATE + 2 + p, p)

            def late_pair(i):
                for k in range(2):
                    g = i * 2 + (EARLY + k)
                    n = i * 8 + (U_LATE + 4 + 4 * k)
                    dve.wait_ge(tile_free, i * 16 + (T_LATE + 8 * (k + 1)))
                    for piece in coefficients(g, (EARLY + k) % 2):
                        piece()
                    ops, end = sparse(i, EARLY + k, K_LATE, 2, S_LATE + K_LATE * k)
                    for op in ops[:4]:
                        op()
                    make_lo(n, 0)
                    for op in ops[4:12]:
                        op()
                    make_lo(n + 1, 1)
                    for op in ops[12:LATE_AHEAD]:
                        op()
                    gather_out(g, n + 2, ops[LATE_AHEAD:])
                    end()

            repeat(0, (NGRP - 1 - EARLY) // 2, 8, late_pair)
            dve.wait_ge(tile_free, T_LATE + 8 * (NGRP - EARLY))
            for piece in coefficients(NGRP - 1, (NGRP - 1) % 2):
                piece()

            def close(n, b):
                if not n:
                    dve.wait_ge(par_in, 16 * 6)
                step(V.scalar_tensor_tensor(acc[:, b, :], acc[:, b, :], DESCALE, par_end[:, 0, :], ALU.mult, ALU.mult))
                settle()
                step(V.scalar_tensor_tensor(xt[:, b, :], xt[:, b, :], ALPHA, acc[:, b, :], ALU.mult, ALU.add))
                settle()
                statistics(xt, range(b, b + 1))

            def finish(n, b):
                normalise(5 + n, xt, xt, y_norm, range(b, b + 1))

            dve.wait_ge(weight_ready, NGRP)
            last_rows = list(range(LAG))
            for half in range(2):
                for b in range(DB):
                    t = DB * half + b
                    dve.wait_ge(v_ready, VT * (NGRP - 1) + t + 1)
                    dst = acc[:, b, half * HT:(half + 1) * HT]
                    V.tensor_tensor(dst, psX[t % 4][:, :], dst, ALU.add).then_inc(v_free, 1)
                    if half == 0:
                        for j in last_rows[:3]:
                            m = 2 * SLOTS - LAG + j
                            v_row(SLOTS - LAG + j, m, j % NSP, (m % 4, 16 * (m // 4 + 1)))
                        del last_rows[:3]
                        if b == DB - 1:
                            dve.wait_ge(row_used, 2 * SLOTS)
                            for n in range(NSP):
                                close(n, DB + n)
                                if n:
                                    finish(n - 1, DB + n - 1)
                    else:
                        dve.wait_ge(v_free, VT * (NGRP - 1) + t + 1)
                        close(NSP + b, b)
                        finish(NSP + b - 1, b - 1 if b else NB - 1)
            finish(NB - 1, DB - 1)

        @block.tensor
        def _(pe):
            mm = nc.tensor.matmul

            def aux_tile(a):
                wait(pe, aux_free, a - 3)
                return psX[a % 4]

            def product(ps, lhs, rhs, chunks, between=None):
                n = len(chunks)
                for s, k in enumerate(chunks):
                    mm(ps, lhs[0](k), rhs[0](k), start=(s == 0), stop=False)
                    mm(ps, lhs[0](k), rhs[1](k), start=False, stop=False)
                    last = mm(ps, lhs[1](k), rhs[0](k), start=False, stop=(s == n - 1))
                    if between:
                        between(s)
                return last

            def w_unit(p, columns):
                return [w[:, p, :].rearrange("p (k n) -> p k n", n=columns) for w in (w_hi, w_lo)]

            def feature_unit(n, p, t, hi, lo, between=None, tokens=HT):
                pe.wait_ge(lo_done, n + 1)
                w = w_unit(p, UC)
                for j in range(2):
                    for half in range(2):
                        r = 2 * j + half
                        wait(pe, tile_free, t + (r - 3))
                        product(psU[r][:, 0:tokens],
                                [lambda k, s=s: w[s][:, k, j * P:(j + 1) * P] for s in range(2)],
                                [lambda k, s=s: (hi, lo)[s][:, k, half * tokens:(half + 1) * tokens] for s in range(2)],
                                range(KD), between and (lambda s, r=r: between(r, s))).then_inc(tile_ready, 1)

            def expert_unit(n, p, t, between=None):
                feature_unit(n, p, t, h_hi, h_lo, between, HD)

            def token_unit(n, p, t, hi, lo):
                pe.wait_ge(lo_done, n + 1)
                w = w_unit(p, UC)
                for b in range(NB):
                    wait(pe, tile_free, t + (b - 3))
                    product(psU[b % 4][:, 0:UC],
                            [lambda k, s=s: (hi, lo)[s][:, k, b * P:(b + 1) * P] for s in range(2)],
                            [lambda k, s=s: w[s][:, k, :] for s in range(2)],
                            range(KD)).then_inc(tile_ready, 1)

            def transposes(first, src, half):
                for k in range(KD):
                    ps = aux_tile(first + 8 * half + k)
                    for b in range(4):
                        ins = nc.tensor.transpose(ps[:, b * P:(b + 1) * P], src[:, 4 * half + b, k * P:(k + 1) * P],
                                                  ident[:, :])
                    ins.then_inc(aux_ready, 1)

            def cond_unit(w, a):
                w = w.rearrange("p (k n) -> p k n", k=KD)
                ps = aux_tile(a)
                for k in range(KD):
                    ins = mm(ps[:, 0:UC], crep[:, k, :], w[:, k, :], start=(k == 0), stop=(k == KD - 1))
                ins.then_inc(aux_ready, 1)

            pe.wait_ge(crep_ready, 1)
            for u in range(COND1):
                pe.wait_ge(stage_in[u % 2], 16 * (u // 2 + 1))
                cond_unit(stage[:, u % 2, :], u)
            pe.wait_ge(ident_ready, 2)
            pe.wait_ge(norm_ready, 1)
            for half in range(2):
                transposes(A_HT, xt, half)
            pe.wait_ge(h_split, 16)
            for u in range(N_V):
                token_unit(U_V + u, u % 2, T_V + 8 * u, h_hi, h_lo)
                for r in range(4):
                    pe.wait_ge(cond_in[r], 16 * (u + 1))
                    cond_unit(cond_ring[:, r, :], A_COND2 + 4 * u + r)
            with pe.Fori(0, N_CONV // 2) as i:
                for p in range(2):
                    feature_unit(i * 2 + (U_CONV + p), p, i * 8 + (T_CONV + 4 * p), h_hi, h_lo)
            pe.wait_ge(norm_ready, 2)
            pe.wait_ge(mask_ready, 1)
            for a in range(16):
                g, half = a // 2, a % 2
                ps = aux_tile(A_MIX + a)
                for b in range(4):
                    ins = mm(ps[:, b * P:(b + 1) * P], xt[:, 4 * half + b, g * P:(g + 1) * P], ws_t[:, g, :],
                             start=True, stop=True)
                ins.then_inc(aux_ready, 1)
            with pe.Fori(0, N_U // 2) as i:
                for p in range(2):
                    feature_unit(i * 2 + (U_U + p), p, i * 8 + (T_U + 4 * p), h_hi, h_lo)
            pe.wait_ge(ev_free, E_MERGE)
            with pe.Fori(0, 4) as i:
                for r, (hi, lo) in enumerate(((ya_hi, ya_lo), (h_hi, h_lo), (yb_hi, yb_lo), (h_hi, h_lo))):
                    feature_unit(i * 4 + (U_MERGE + r), r % 2, i * 16 + (T_MERGE + 4 * r), hi, lo)
            pe.wait_ge(ev_free, E_END)
            for u in range(N_O):
                token_unit(U_O + u, u % 2, T_O + 8 * u, m_hi, m_lo)
            for half in range(2):
                pe.wait_ge(norm_ready, 3 + half)
                transposes(A_H2T, x2, half)
            pe.wait_ge(h_split, 32)
            pe.wait_ge(keys_in, 16)

            def heads(i):
                for q in range(2):
                    n, t = i * 6 + (U_Q + 3 * q), i * 24 + (T_Q + 12 * q)
                    feature_unit(n, q, t, h_hi, h_lo)
                    pe.wait_ge(tile_free, t + 4)
                    for b2 in range(4):
                        wait(pe, sc_free, i * 8 + (4 * (q - 1) + b2 + 1))
                        for m in range(4):
                            b, half = 2 * b2 + m // 2, m % 2
                            keys = keys_sb[:, bass.ds(i * 4 + (2 * q + half), 1), :].rearrange("p a k -> p (a k)")
                            ins = mm(psX[b2][:, m * P:(m + 1) * P], qb[q][:, half, b * P:(b + 1) * P], keys,
                                     start=True, stop=True)
                        ins.then_inc(sc_ready, 1)
                    for e in range(2):
                        expert_unit(n + (1 + e), (q + 1 + e) % 2, t + (4 + 4 * e))

            heads(0)
            with pe.Fori(1, HEADS // 2) as i:
                heads(i)
            for k in range(3):
                expert_unit(U_TAIL + k, k % 2, T_TAIL + 4 * k)
            pe.wait_ge(gate_ready, 1)
            pe.wait_ge(sc_free, 4 * HEADS)
            for a in range(6):
                kind, half = a // 2, a % 2
                ps = aux_tile(A_IDX + a)
                src = (i1_all, i2_all, s_all)[kind].rearrange("p b h k -> p b (h k)")
                for b in range(4):
                    ins = nc.tensor.transpose(ps[:, b * P:(b + 1) * P], src[:, 4 * half + b, :], ident[:, :])
                ins.then_inc(aux_ready, 1)
            for k in range(3, N_TAIL):
                expert_unit(U_TAIL + k, k % 2, T_TAIL + 4 * k)
            pe.wait_ge(aux_free, A_END)

            def spread(i):
                for u in range(2):
                    def gates(r, s):
                        if s % 2:
                            return
                        q = s // 2
                        at = 16 * u + 4 * r + q
                        wait(pe, g_free, i * 32 + (at - 3))
                        pe.wait_ge(oh_ready, i * 32 + (at + 1))
                        for t in range(4):
                            for c in range(2):
                                ins = mm(psX[q][:, t * P:(t + 1) * P], oh_keys[:, q, 0, :, t],
                                         oh_gate[:, q, c, :, t], start=(c == 0), stop=(c == 1))
                        ins.then_inc(g_ready, 1)
                    expert_unit(i * 2 + (U_SPREAD + u), u, i * 8 + (T_SPREAD + 4 * u), gates)

            spread(0)
            with pe.Fori(1, N_SPREAD // 2) as i:
                spread(i)
            for k in range(N_POST):
                expert_unit(U_POST + k, k % 2, T_POST + 4 * k)
            pe.wait_ge(g_free, DT // 4)

            def expert_out(n, c, p, first=False):
                pe.wait_ge(a_free, c + 1)
                for half in range(2):
                    pe.wait_ge(lo_done, n + (half + 1))
                    w = w_unit(half, HT)
                    for b in range(DB):
                        t = DB * half + b
                        if not (first and t < 4):
                            pe.wait_ge(v_free, c * VT + (t - 3))
                        product(psX[t % 4][:, :],
                                [lambda k, s=s: (c_hi, c_lo)[s][p][:, k, b * P:(b + 1) * P] for s in range(2)],
                                [lambda k, s=s: w[s][:, k, :] for s in range(2)],
                                range(4)).then_inc(v_ready, 1)

            def expert_in(n, t):
                for half in range(2):
                    expert_unit(n + half, half, t + 4 * half)

            expert_out(U_VE, 0, 0, True)
            with pe.Fori(0, (EARLY - 1) // 2) as i:
                for p in range(2):
                    expert_out(i * 4 + (U_VE + 2 * (p + 1)), i * 2 + (p + 1), 1 - p)
            expert_in(U_LATE, T_LATE)
            with pe.Fori(0, (NGRP - 1 - EARLY) // 2) as i:
                for k in range(2):
                    expert_in(i * 8 + (U_LATE + 2 + 4 * k), i * 16 + (T_LATE + 8 * (k + 1)))
                    expert_out(i * 8 + (U_LATE + 4 + 4 * k), i * 2 + (EARLY + k), (EARLY + k) % 2)
            expert_out(U_LAST, NGRP - 1, (NGRP - 1) % 2)


def _unit_columns(w):
    return w.reshape(KD, P, -1, UC).transpose(2, 1, 0, 3)


def kernel(**inputs):
    import concourse.bacc as _bacc
    from concourse.bass_utils import run_bass_kernel_spmd as _run

    a = {k: np.asarray(v) for k, v in inputs.items()}
    w_in = _unit_columns(a["w_in"][0])
    part = {name: w_in[4 * i:4 * i + 4] for i, name in enumerate(("u", "v", "gB", "gC", "z", "ga", "gb"))}
    pa, pb = _unit_columns(a["p_a"][0]), _unit_columns(a["p_b"][0])
    order = list(part["v"])
    for q in range(4):
        order += [part["z"][q], part["gC"][q], part["gB"][q]]
    order += list(part["u"])
    for q in range(4):
        order += [pa[q], part["ga"][q], pb[q], part["gb"][q]]
    order += list(_unit_columns(a["w_o"][0])) + list(_unit_columns(a["w_q_peer"][0]))
    arrays = {
        "x": a["x"][0],
        "c_col": a["c"].reshape(KD, P).T,
        "w_cond": _unit_columns(a["w_cond"][0]).reshape(NCOND, P, 2048),
        "b_cond": a["b_cond"][0],
        "w_front": np.stack(order),
        "ln_g": a["gmlp_ln_g"][0],
        "ln_b": a["gmlp_ln_b"][0],
        "w_spat": a["w_spatial"][0].transpose(2, 0, 1),
        "b_spat": a["b_spatial"][0].reshape(-1),
        "conv_w": a["conv_w"][0].reshape(3, KD, P).transpose(2, 1, 0),
        "ln1_g": a["ln1_g"][0],
        "ln1_b": a["ln1_b"][0],
        "keys_t": a["sub_keys"][0].reshape(2 * HEADS, NKEYS, P).transpose(2, 0, 1),
        "u_units": a["expert_u"][0].reshape(P, NGRP, 2, 2, KD, P).transpose(1, 2, 5, 4, 3, 0).reshape(2 * NGRP, P, 2048),
        "u_rows": a["expert_u"][0],
        "expert_v": a["expert_v"][0],
        "ln2_g": a["ln2_g"][0],
        "ln2_b": a["ln2_b"][0],
    }
    nc = _bacc.Bacc("TRN2", target_bir_lowering=False, num_devices=1)
    arrays = {"in_" + k: np.ascontiguousarray(v) for k, v in arrays.items()}
    args = [nc.dram_tensor(k, v.shape, mybir.dt.from_np(v.dtype), kind="ExternalInput").ap() for k, v in arrays.items()]
    names = [k[3:] for k in arrays]
    args.insert(names.index("expert_v") + 1, args[names.index("expert_v")])
    args[names.index("expert_v")] = args[names.index("expert_v")].rearrange("(p g j) d -> g p j d", p=P, j=4)
    out = nc.dram_tensor("out", (S, D), F32, kind="ExternalOutput").ap()
    trunk_layer(nc, *args, out)
    r = _run(nc, [arrays], core_ids=[0])
    return r.results[0]["out"].reshape(1, S, D)
```
